# Optimizing a Trainium2 kernel written in Bass

```python
import jax, jax.numpy as jnp
from jax import lax
import numpy as np

D_MODEL = 1024
BATCH = 1
SEQ = 1024
DEPTH = 1
DEC_BATCH = 8
DEC_SEQ = 16
PAST_LEN = 128

CHUNK = 64
WINDOW = 128
W_CHUNKS = WINDOW // CHUNK
HEAD_DIM = 64
N_HEADS = D_MODEL // HEAD_DIM
N_KV_HEADS = 4
GROUP = N_HEADS // N_KV_HEADS
Q_DIM = N_HEADS * HEAD_DIM
KV_DIM = N_KV_HEADS * HEAD_DIM
D_CONV = D_MODEL
CONV_W = 3
D_FF = ((8 * D_MODEL // 3 + 255) // 256) * 256
EPS = 1e-6
NEG_INF = -1e30
SCALE = HEAD_DIM ** -0.5
SPLITS = list(np.cumsum([D_CONV, D_CONV, D_CONV, Q_DIM, KV_DIM, KV_DIM, D_MODEL]))
IN_COLS = 3 * D_CONV + Q_DIM + 2 * KV_DIM + 2 * D_MODEL

kernel_name = "hybrid_shortconv_swa_sink_stream_step"

def rms_norm(x, w):
    xf = x.astype(jnp.float32)
    y = xf * lax.rsqrt(jnp.mean(xf * xf, axis=-1, keepdims=True) + EPS)
    return (y * w.astype(jnp.float32)).astype(x.dtype)

def mixer_inputs(x, norm_w, w_in, q_norm_w, k_norm_w):
    b, t = x.shape[:2]
    xn = rms_norm(x, norm_w)
    h, gb, gc, q, k, v, g_conv, g_attn = jnp.split(xn @ w_in, SPLITS, axis=-1)
    q = rms_norm(q.reshape(b, t, N_KV_HEADS, GROUP, HEAD_DIM), q_norm_w)
    k = rms_norm(k.reshape(b, t, N_KV_HEADS, HEAD_DIM), k_norm_w)
    v = v.reshape(b, t, N_KV_HEADS, HEAD_DIM)
    u = gc * h
    return u, gb, q, k, v, g_conv, g_attn

def causal_conv(u, prefix, w):
    t = u.shape[1]
    up = jnp.concatenate([prefix, u], axis=1)
    y = w[0] * up[:, 0:t] + w[1] * up[:, 1:t + 1] + w[2] * up[:, 2:t + 2]
    return y, up[:, -(CONV_W - 1):]

def sink_attention(q, k, v, valid, sinks):
    s = jnp.einsum('bcqhgd,bckhd->bchgqk', q, k).astype(jnp.float32) * SCALE
    s = jnp.where(valid, s, NEG_INF)
    sink = jnp.broadcast_to(sinks.astype(jnp.float32).reshape(N_KV_HEADS, GROUP)[None, None, :, :, None, None],
                            s.shape[:-1] + (1,))
    p = jax.nn.softmax(jnp.concatenate([s, sink], axis=-1), axis=-1)[..., :-1]
    return jnp.einsum('bchgqk,bckhd->bcqhgd', p.astype(v.dtype), v)

def window_attention_prompt(q, k, v, sinks):
    b, t = q.shape[:2]
    nc = t // CHUNK
    qc = q.reshape(b, nc, CHUNK, N_KV_HEADS, GROUP, HEAD_DIM)

    def band(a):
        ac = a.reshape(b, nc, CHUNK, N_KV_HEADS, HEAD_DIM)
        ap = jnp.pad(ac, ((0, 0), (W_CHUNKS, 0), (0, 0), (0, 0), (0, 0)))
        return jnp.concatenate([ap[:, j:j + nc] for j in range(W_CHUNKS + 1)], axis=2)

    kb, vb = band(k), band(v)
    chunk_idx = jnp.arange(nc)[:, None]
    src_off = jnp.repeat(jnp.arange(W_CHUNKS + 1), CHUNK)[None, :]
    valid = (chunk_idx + src_off - W_CHUNKS >= 0)[None, :, None, None, None, :]
    o = sink_attention(qc, kb, vb, valid, sinks)
    return o.reshape(b, t, Q_DIM)

def window_attention_sample(q, k, v, cache_k, cache_v, sinks):
    b, t = q.shape[:2]
    kk = jnp.concatenate([cache_k, k], axis=1)[:, None]
    vv = jnp.concatenate([cache_v, v], axis=1)[:, None]
    o = sink_attention(q[:, None], kk, vv, jnp.ones((), dtype=bool), sinks)
    return o[:, 0].reshape(b, t, Q_DIM)

def block_output(x, y_conv, y_attn, g_conv, g_attn, w_out, norm_ffn_w, w_gate, w_up, w_down):
    merged = jax.nn.sigmoid(g_conv) * y_conv + jax.nn.sigmoid(g_attn) * y_attn
    x = x + merged @ w_out
    xn = rms_norm(x, norm_ffn_w)
    return x + (jax.nn.silu(xn @ w_gate) * (xn @ w_up)) @ w_down

def setup_inputs(seed: int = 0) -> dict:
    key = jax.random.key(seed)
    ks = jax.random.split(key, 18)
    f32 = jnp.float32
    cache_len = min(WINDOW, PAST_LEN)
    nrm = lambda k, shape, s: jax.random.normal(k, shape, f32) * s
    return {
        "x_prompt": nrm(ks[0], (BATCH, SEQ, D_MODEL), 1.0),
        "x_sample": nrm(ks[1], (DEC_BATCH, DEC_SEQ, D_MODEL), 1.0),
        "state_conv": nrm(ks[2], (DEPTH, DEC_BATCH, CONV_W - 1, D_CONV), 1.0),
        "cache_k": nrm(ks[3], (DEPTH, DEC_BATCH, cache_len, N_KV_HEADS, HEAD_DIM), 1.0),
        "cache_v": nrm(ks[4], (DEPTH, DEC_BATCH, cache_len, N_KV_HEADS, HEAD_DIM), 1.0),
        "norm_mix_w": 1.0 + nrm(ks[5], (DEPTH, D_MODEL), 0.02),
        "w_in": nrm(ks[6], (DEPTH, D_MODEL, IN_COLS), D_MODEL ** -0.5),
        "conv_w": nrm(ks[7], (DEPTH, CONV_W, D_CONV), CONV_W ** -0.5),
        "q_norm_w": 1.0 + nrm(ks[8], (DEPTH, HEAD_DIM), 0.02),
        "k_norm_w": 1.0 + nrm(ks[9], (DEPTH, HEAD_DIM), 0.02),
        "sinks": nrm(ks[10], (DEPTH, N_HEADS), 0.5),
        "w_out": nrm(ks[11], (DEPTH, D_MODEL, D_MODEL), D_MODEL ** -0.5),
        "norm_ffn_w": 1.0 + nrm(ks[12], (DEPTH, D_MODEL), 0.02),
        "w_gate": nrm(ks[13], (DEPTH, D_MODEL, D_FF), D_MODEL ** -0.5),
        "w_up": nrm(ks[14], (DEPTH, D_MODEL, D_FF), D_MODEL ** -0.5),
        "w_down": nrm(ks[15], (DEPTH, D_FF, D_MODEL), D_FF ** -0.5),
    }

def reference(x_prompt, x_sample, state_conv, cache_k, cache_v, norm_mix_w, w_in, conv_w,
              q_norm_w, k_norm_w, sinks, w_out, norm_ffn_w, w_gate, w_up, w_down):
    yp, ys = x_prompt, x_sample
    conv_p, k_p, v_p, conv_s, k_s, v_s = [], [], [], [], [], []
    for l in range(DEPTH):
        u, gb, q, k, v, g_c, g_a = mixer_inputs(yp, norm_mix_w[l], w_in[l], q_norm_w[l], k_norm_w[l])
        zero_prefix = jnp.zeros((u.shape[0], CONV_W - 1, D_CONV), u.dtype)
        cy, ctail = causal_conv(u, zero_prefix, conv_w[l])
        ay = window_attention_prompt(q, k, v, sinks[l])
        yp = block_output(yp, gb * cy, ay, g_c, g_a, w_out[l], norm_ffn_w[l], w_gate[l], w_up[l], w_down[l])
        conv_p.append(ctail)
        k_p.append(k[:, -WINDOW:])
        v_p.append(v[:, -WINDOW:])
        u, gb, q, k, v, g_c, g_a = mixer_inputs(ys, norm_mix_w[l], w_in[l], q_norm_w[l], k_norm_w[l])
        cy, ctail = causal_conv(u, state_conv[l].astype(u.dtype), conv_w[l])
        ay = window_attention_sample(q, k, v, cache_k[l].astype(k.dtype), cache_v[l].astype(v.dtype), sinks[l])
        ys = block_output(ys, gb * cy, ay, g_c, g_a, w_out[l], norm_ffn_w[l], w_gate[l], w_up[l], w_down[l])
        conv_s.append(ctail)
        k_s.append(k)
        v_s.append(v)
    return (yp, ys, jnp.stack(conv_p), jnp.stack(k_p), jnp.stack(v_p),
            jnp.stack(conv_s), jnp.stack(k_s), jnp.stack(v_s))


_drawn_inputs = setup_inputs


def setup_inputs(seed=0):
    import zlib

    import numpy as np

    out = dict(_drawn_inputs(seed))
    spreads = {}
    factors = {'q_norm_w': 8.0, 'sinks': 64.0, 'norm_ffn_w': 4.287}
    for name, (base, spread) in spreads.items():
        noise = np.random.default_rng([zlib.crc32(name.encode()), seed]).standard_normal(out[name].shape)
        drawn = base * np.exp(spread * noise) if base else spread * noise
        out[name] = __import__('jax').numpy.asarray(drawn.astype(out[name].dtype))
    for name, factor in factors.items():
        out[name] = (out[name] * factor).astype(out[name].dtype)
    return out
```

```python
from contextlib import ExitStack

import numpy as np

import concourse.bass as bass
from concourse import mybir

F32, F32R, BF16 = mybir.dt.float32, mybir.dt.float32r, mybir.dt.bfloat16
ALU = mybir.AluOpType
ACT = mybir.ActivationFunctionType
AX_X = mybir.AxisListType.X

P = 128
D = 1024
SEQ = 1024
DEC_B, DEC_T = 8, 16
TOK = SEQ + DEC_B * DEC_T
NT = TOK // P
NG = 3
G = TOK // NG
KT = D // P
HD = 64
NH, NKV = D // HD, 4
D_FF = 2816
FC = 256
NCH = D_FF // FC
EPS = 1e-6
NEG = -1e30
H_OFF, B_OFF, C_OFF, Q_OFF = 0, D, 2 * D, 3 * D
K_OFF = 4 * D
V_OFF = K_OFF + NKV * HD
GC_OFF = V_OFF + NKV * HD
GA_OFF = GC_OFF + D
UP0 = 2 + SEQ
UW = UP0 + DEC_B * (2 + DEC_T)
SLAB = KT * P
Q_SLAB = 4
PAIR_SLAB = 12
OUT_SLAB = 52
FFN_SLAB = 60
STEPS = 8
SLOTS = 3 * STEPS
PASSES = ((0, 0), (0, 1), (1, 0))
DU = 5


class Slab:

    def __init__(self, first, per=0, i=0):
        self.n = first + per * i
        self.slot = first % 2
        self.turn = first // 2 + (per // 2) * i


def build(nc, io):
    ctx = ExitStack()
    with ctx:
        def sb(name, shape, dt=F32):
            return ctx.enter_context(nc.sbuf_tensor(name, shape, dt))

        def sem(name):
            return ctx.enter_context(nc.semaphore(name))

        def overlay(name, nbytes, *groups):
            out = []
            for group in groups:
                with ExitStack() as inner:
                    out.append([inner.enter_context(nc.sbuf_tensor(n, s, d)) for n, s, d in group])
            ctx.enter_context(nc.sbuf_tensor(name, [P, nbytes // 4], F32))
            return out

        xs = [sb("x_hi", [P, KT, TOK], F32R), sb("x_lo", [P, KT, TOK], F32R)]
        ([O], [xn_f, scratch_f, wbc_f, Gt, Ht]) = overlay(
            "o_space", KT * TOK * 4,
            [("O", [P, KT, TOK], F32)],
            [("xn_f", [P, 2, D], F32), ("scratch_f", [P, D], F32), ("wbc_f", [P, D], F32),
             ("silu_gate", [P, 2, TOK], F32), ("ffn_h", [P, 2, G], F32)])
        ([X], [V, kT, qst, kst, vst, ck, cv, ks, ksmp, vsmp, qs, mask, window, halves, ones_row]) = overlay(
            "x_space", NT * D * 4,
            [("X", [P, NT, D], F32)],
            [("V", [P, NT + 1, NKV * HD], F32), ("kT", [P, 2, P + TOK], F32),
             ("q_stage", [P, 2, 4, P], F32), ("k_stage", [P, 2, 2 * P], F32), ("v_stage", [P, 2, 2, P], F32),
             ("cache_k_rows", [P, 2, P], F32), ("cache_v_rows", [P, 2, P], F32), ("cache_kT", [P, 2, P], F32),
             ("sample_kT", [P, P], F32), ("sample_v", [P, P], F32), ("q_sample", [P, 2, 4, DEC_T], F32),
             ("mask", [2, 2, 2 * P], BF16), ("window", [1, 2 * P - DEC_T], BF16),
             ("halves", [2, P], BF16), ("ones_row", [1, P], BF16)])
        act_bytes = 2 * 2 * TOK * 4
        ([xn_p, scratch_p, wbc_p, blockones], [Pb, PT, sqst, sqs], [act0]) = overlay(
            "act0_space", act_bytes,
            [("xn_p", [P, 2, D], F32), ("scratch_p", [P, D], F32), ("wbc_p", [P, D], F32), ("blockones", [P, P], F32)],
            [("probs", [P, 4, 2 * P], F32), ("probsT", [P, 2, 4, P], F32), ("q_sq", [P, 4, P], F32),
             ("q_sample_sq", [P, 4, DEC_T], F32)],
            [("act0", [P, 2, 2, TOK], F32R)])
        ([A, U, S, Rk], [act1]) = overlay(
            "act1_space", act_bytes,
            [("branch", [P, 2, TOK], F32), ("u", [P, UW], F32), ("gate", [P, 2, G], F32), ("unused", [P, 4], F32)],
            [("act1", [P, 2, 2, TOK], F32R)])
        acts = [act0, act1]
        raw = [sb(f"w_raw{i}", [P, SLAB]) for i in range(2)]
        ws = [[sb(f"w_hi{i}", [P, SLAB], F32R), sb(f"w_lo{i}", [P, SLAB], F32R)] for i in range(2)]
        ident = sb("ident", [P, P])
        ones2 = sb("ones2", [P, 2])
        tails = sb("tails", [P, KT, 2 + 2 * DEC_B])
        stT = sb("stT", [P, DEC_B, 2, KT])
        cwT = sb("cwT", [P, 3, KT])
        qnw = sb("qnw", [P, 1])
        knw = sb("knw", [P, 1])
        eps = sb("eps", [P, 1])
        sinkb = sb("sinkb", [P, NH])
        sinkS = sb("sinkS", [P, 2])
        neghalf = sb("neghalf", [P, 9])
        ss = sb("ss", [P, NT])
        sd = sb("sd", [P, NT])
        rms = sb("rms", [P, NT])
        ms = sb("ms", [P, 2, 9])
        rs = sb("rs", [P, 2, 9])
        soft = sb("soft", [P, 9, 4])
        kr = A[:, 0, :].rearrange("p (r g) -> p r g", r=NG)
        kout = A[:, 1, 0:4 * P].rearrange("p (t c) -> p t c", t=2)
        rows_st, rows_cw = A[:, 0, 0:P], A[0:24, 0, P:2 * P]
        tout = U[0:2 + 2 * DEC_B, 0:D]

        banks = ctx.enter_context(nc.psum_tensor("banks", [P, 8, 512], F32))
        scores = banks[:, 3:5, :].rearrange("p b (h k) -> p (b h) k", k=2 * P)

        const_in = sem("const_in")
        x_in = [sem(f"x_in{t}") for t in range(NT)]
        raw_in = [sem("raw_in0"), sem("raw_in1")]
        cache_in = [sem("cache_in0"), sem("cache_in1")]
        wbc_in = sem("wbc_in")
        consts_made = sem("consts_made")
        w_hi, w_lo = sem("w_hi_ready"), sem("w_lo_ready")
        sq_done, sd_done, rms_done, xn_ready = sem("sq_done"), sem("sd_done"), sem("rms_done"), sem("xn_ready")
        nT_done, norm_hi, norm_lo = sem("nT_done"), sem("norm_hi"), sem("norm_lo")
        gemm_ready = sem("gemm_ready")
        bank_free = [sem(f"bank_free{g}") for g in range(NG)]
        smallT, small_done = sem("smallT"), sem("small_done")
        vt_ready, v_done = sem("vt_ready"), sem("v_done")
        k_ms, k_sd, k_rs = sem("k_ms"), sem("k_sd"), sem("k_rs")
        kt_ready, kout_done, kq_done = sem("kt_ready"), sem("kout_done"), sem("kq_done")
        pads_done, masks_done = sem("pads_done"), sem("masks_done")
        staged = sem("staged")
        s0_done, s0_used, rs_ready = sem("s0_done"), sem("s0_used"), sem("rs_ready")
        s1_done, s2_done, s3_done = sem("scores_done"), sem("probsT_done"), sem("pv_done")
        soft_done, exp_done, p_ready = sem("soft_done"), sem("exp_done"), sem("p_ready")
        pt_v, pt_a, o_done = sem("pt_v"), sem("pt_a"), sem("o_done")
        conv_step, sg_used, merged = sem("conv_step"), sem("sg_used"), sem("merged")
        tail_step, tailsT, tout_done = sem("tail_step"), sem("tailsT"), sem("tout_done")
        m_hi, m_lo = sem("m_hi"), sem("m_lo")
        d_ready, d_free = sem("d_ready"), sem("d_free")
        f_hi, f_lo = sem("f_hi"), sem("f_lo")
        small_out, y_out = sem("small_out"), sem("y_out")

        w_in = io["w_in"][0].rearrange("(k p) c -> p k c", p=P)
        w_q = io["w_in"][0][:, Q_OFF:Q_OFF + D].rearrange("(k p) (a s j d) -> p k a s j d", p=P, a=2, s=2, j=4)
        w_gate = io["w_gate"][0].rearrange("(k p) c -> p k c", p=P)
        w_up = io["w_up"][0].rearrange("(k p) c -> p k c", p=P)
        w_out = io["w_out"][0].rearrange("(k p) n -> p k n", p=P)
        w_down = io["w_down"][0].rearrange("(k p) n -> p k n", p=P)
        xp = io["x_prompt"][0].rearrange("(t p) d -> t p d", p=P)
        xsm = io["x_sample"].rearrange("b t d -> (b t) d")
        yp = io["y_prompt"][0].rearrange("(t p) d -> t p d", p=P)
        ysm = io["y_sample"].rearrange("b t d -> (b t) d")
        cache_k = io["cache_k"][0].rearrange("b n h d -> b n (h d)")
        cache_v = io["cache_v"][0].rearrange("b n h d -> b n (h d)")

        def slab_is_done(eng, kind, idx):
            if kind == "f":
                eng.wait_ge(gemm_ready, 3 * (idx + 1))
            else:
                eng.wait_ge(d_ready, NT * (idx + 1))

        block = ctx.enter_context(nc.Block())

        @block.sync
        def _(sp):
            def load(slab, halves_of):
                if not (isinstance(slab.n, int) and slab.n < 2):
                    sp.wait_ge(w_lo, slab.n - 1)
                for dst, src in halves_of:
                    sp.dma_start(dst, src).then_inc(raw_in[slab.slot], 16)

            def cols(slab, w, c0):
                dst = raw[slab.slot][:, :].rearrange("p (k c) -> p k c", k=KT)
                load(slab, [(dst[:, h:h + 4, :], w[:, h:h + 4, bass.ds(c0, P)]) for h in (0, 4)])

            sp.dma_start(X[:, 0, :], xp[0]).then_inc(x_in[0], 16)
            sp.dma_start(wbc_p[:, :], io["norm_mix_w"][0].partition_broadcast(P)).then_inc(wbc_in, 16)
            sp.dma_start(X[:, 1, :], xp[1]).then_inc(x_in[1], 16)
            cols(Slab(0), w_in, V_OFF)
            for t in range(2, 5):
                sp.dma_start(X[:, t, :], xp[t]).then_inc(x_in[t], 16)
            cols(Slab(1), w_in, V_OFF + P)
            for t in range(5, NT):
                sp.dma_start(X[:, t, :], xp[t] if t < NT - 1 else xsm).then_inc(x_in[t], 16)
            cols(Slab(2), w_in, K_OFF)
            cols(Slab(3), w_in, K_OFF + P)
            with sp.Fori(0, 2) as i:
                for j in range(4):
                    slab = Slab(Q_SLAB + j, 4, i)
                    dst = raw[slab.slot][:, :].rearrange("p (k s c) -> p k s c", k=KT, s=2)
                    load(slab, [(dst[:, :, h, :], w_q[:, :, bass.ds(i, 1), h, j, :].rearrange("p k a d -> p k (a d)"))
                                for h in range(2)])

            def pair_loads(i):
                for jj in range(2):
                    for c, off in enumerate((H_OFF, C_OFF, B_OFF, GC_OFF)):
                        cols(Slab(PAIR_SLAB + 4 * jj + c, 10, i), w_in, off + (2 * i + jj) * P)
                for jj in range(2):
                    cols(Slab(PAIR_SLAB + 8 + jj, 10, i), w_in, GA_OFF + (2 * i + jj) * P)

            with sp.Fori(0, 2) as i:
                pair_loads(i)
            with sp.Fori(2, 4) as i:
                pair_loads(i)

            def rows(slab, w, k0, hf):
                load(slab, [(raw[slab.slot][:, k * 512:(k + 1) * 512],
                             w[:, bass.ds(k0 + k, 1), hf * 512:(hf + 1) * 512].rearrange("p a c -> p (a c)"))
                            for k in range(2)])

            sp.wait_ge(o_done, 2 * SLOTS)
            sp.wait_ge(small_out, 64)
            for t in range(NT):
                sp.dma_start(X[:, t, :], xp[t] if t < NT - 1 else xsm).then_inc(x_in[t], 16)
            for c in range(4):
                for hf in range(2):
                    rows(Slab(OUT_SLAB + 2 * c + hf), w_out, 2 * c, hf)
            sp.wait_ge(m_lo, 4)
            sp.dma_start(wbc_f[:, :], io["norm_ffn_w"][0].partition_broadcast(P)).then_inc(wbc_in, 16)

            def gate_up(first, per, i, c):
                for b in range(2):
                    cols(Slab(first + 2 * b, per, i), w_gate, c * FC + b * P)
                    cols(Slab(first + 2 * b + 1, per, i), w_up, c * FC + b * P)

            def down(first, per, i, c):
                for hf in range(2):
                    rows(Slab(first + hf, per, i), w_down, 2 * c, hf)

            gate_up(FFN_SLAB, 0, 0, 0)
            with sp.Fori(0, (NCH - 1) // 2) as i:
                gate_up(FFN_SLAB + 4, 12, i, 2 * i + 1)
                down(FFN_SLAB + 8, 12, i, 2 * i)
                gate_up(FFN_SLAB + 10, 12, i, 2 * i + 2)
                down(FFN_SLAB + 14, 12, i, 2 * i + 1)
            down(FFN_SLAB + 64, 0, 0, NCH - 1)
            for hf in range(2):
                for t in range(NT):
                    sp.wait_ge(d_free, NT * (8 + 2 * (NCH - 1) + hf) + t + 1)
                    dst = yp[t] if t < NT - 1 else ysm
                    sp.dma_start(dst[:, hf * 512:(hf + 1) * 512], X[:, t, hf * 512:(hf + 1) * 512]).then_inc(y_out, 16)
            sp.wait_ge(y_out, 16 * 2 * NT)

        @block.gpsimd
        def _(gp):
            gp.dma_start(rows_st, io["state_conv"][0].rearrange("b r (j c) -> (b r j) c", c=P)).then_inc(const_in, 16)
            gp.dma_start(rows_cw, io["conv_w"][0].rearrange("w (j c) -> (w j) c", c=P)).then_inc(const_in, 16)
            for s in range(2):
                gp.dma_start(qnw[HD * s:HD * (s + 1), :], io["q_norm_w"].rearrange("a d -> d a")).then_inc(const_in, 16)
                gp.dma_start(knw[HD * s:HD * (s + 1), :], io["k_norm_w"].rearrange("a d -> d a")).then_inc(const_in, 16)
            gp.dma_start(sinkb[:, :], io["sinks"][0].partition_broadcast(P)).then_inc(const_in, 16)
            sink_rows = io["sinks"][0].rearrange("(a r) -> r a", a=2)
            for r in range(8):
                gp.dma_start(sinkS[DEC_T * r:DEC_T * (r + 1), :], sink_rows[r].partition_broadcast(DEC_T),
                             allow_slow_non_contiguous=True).then_inc(const_in, 16)
            gp.memset(ident[:, :], 0.0).then_inc(consts_made, 1)
            gp.wait_ge(consts_made, 1)
            gp.affine_select(out=ident[:, :], in_=ident[:, :], compare_op=ALU.not_equal, fill=1.0, base=0,
                             pattern=[[-1, P]], channel_multiplier=1).then_inc(consts_made, 1)
            gp.memset(eps[:, :], EPS).then_inc(consts_made, 1)
            gp.memset(blockones[:, :], 0.0).then_inc(consts_made, 1)
            gp.memset(ones2[:, :], 0.0).then_inc(consts_made, 1)
            gp.memset(neghalf[:, :], -0.5).then_inc(consts_made, 1)
            gp.wait_ge(consts_made, 6)
            for s in range(2):
                half = slice(HD * s, HD * (s + 1))
                gp.memset(blockones[half, half], 1.0).then_inc(consts_made, 1)
                gp.memset(ones2[half, s:s + 1], 1.0).then_inc(consts_made, 1)

            def split_lo(slab):
                gp.wait_ge(w_hi, slab.n + 1)
                gp.tensor_tensor(ws[slab.slot][1][:, :], raw[slab.slot][:, :], ws[slab.slot][0][:, :].bitcast(F32),
                                 ALU.subtract).then_inc(w_lo, 1)

            for n in range(3):
                split_lo(Slab(n))
            gp.wait_ge(norm_lo, 2 * NT)
            gp.memset(V[:, 0, :], 0.0).then_inc(pads_done, 1)
            for a in range(2):
                gp.memset(kT[:, a, 0:P], 0.0).then_inc(pads_done, 1)
            gp.memset(mask[:, :, :], 0.0).then_inc(masks_done, 1)
            gp.memset(halves[:, :], 1.0).then_inc(masks_done, 1)
            gp.memset(ones_row[:, :], 1.0).then_inc(masks_done, 1)
            gp.memset(window[:, :], NEG).then_inc(masks_done, 1)
            gp.wait_ge(masks_done, 4)
            gp.affine_select(out=mask[:, 1, :], in_=mask[:, 1, :], compare_op=ALU.is_ge, fill=NEG, base=0,
                             pattern=[[1, 2 * P]], channel_multiplier=-HD).then_inc(masks_done, 1)
            gp.affine_select(out=mask[:, 0, :], in_=mask[:, 0, :], compare_op=ALU.is_ge, fill=NEG, base=-P,
                             pattern=[[1, 2 * P]], channel_multiplier=0).then_inc(masks_done, 1)
            gp.affine_select(out=halves[:, :], in_=halves[:, :], compare_op=ALU.is_ge, fill=0.0, base=0,
                             pattern=[[1, P]], channel_multiplier=-HD).then_inc(masks_done, 1)
            gp.memset(window[:, P - DEC_T:P], 0.0).then_inc(masks_done, 1)
            gp.wait_ge(masks_done, 8)
            for v in range(2):
                gp.affine_select(out=mask[:, v, :], in_=mask[:, v, :], compare_op=ALU.is_ge, fill=NEG, base=3 * HD - 1,
                                 pattern=[[-1, 2 * P]], channel_multiplier=HD).then_inc(masks_done, 1)
            gp.affine_select(out=halves[:, :], in_=halves[:, :], compare_op=ALU.is_ge, fill=0.0, base=HD - 1,
                             pattern=[[-1, P]], channel_multiplier=HD).then_inc(masks_done, 1)
            split_lo(Slab(3))
            split_lo(Slab(4))
            gp.wait_ge(v_done, 6)
            gp.dma_start(io["new_v_prompt"][0, 0].rearrange("n h d -> n (h d)"), V[:, NT - 1, :]).then_inc(small_out, 16)
            gp.dma_start(io["new_v_sample"][0].rearrange("b n h d -> (b n) (h d)"), V[:, NT, :]).then_inc(small_out, 16)
            with gp.Fori(0, 2) as i:
                for j in range(4):
                    split_lo(Slab(Q_SLAB + j + 1, 4, i))
            gp.wait_ge(kout_done, 1)
            gp.dma_start(io["new_k_prompt"][0, 0].rearrange("n h d -> n (h d)"), kout[:, 0, :]).then_inc(small_out, 16)
            gp.dma_start(io["new_k_sample"][0].rearrange("b n h d -> (b n) (h d)"), kout[:, 1, :]).then_inc(small_out, 16)

            def stage(i, t):
                par, q = t % 2, STEPS * i + t
                if t >= 1:
                    gp.wait_ge(s0_done, q)
                if t >= 2:
                    gp.wait_ge(s3_done, 3 * (q - 1))
                for cache, dst in ((cache_k, ck), (cache_v, cv)):
                    gp.dma_start(dst[:, par, :], cache[t][:, bass.ds(i * P, P)]).then_inc(cache_in[par], 16)
                blocks = bass.ds(4 * i, 4)
                q_t = O[:, blocks, t * P:(t + 1) * P]
                q_s = O[:, blocks, SEQ + t * DEC_T:SEQ + (t + 1) * DEC_T]
                gp.tensor_copy(qst[:, par, :, :], q_t)
                gp.tensor_tensor(sqst[:, :, :], q_t, q_t, ALU.mult)
                gp.tensor_copy(qs[:, par, :, :], q_s)
                gp.tensor_tensor(sqs[:, :, :], q_s, q_s, ALU.mult)
                gp.tensor_copy(kst[:, par, :], kT[:, bass.ds(i, 1), t * P:(t + 2) * P].rearrange("p a k -> p (a k)"))
                if t == 0:
                    gp.tensor_copy(ksmp[:, :], kT[:, bass.ds(i, 1), SEQ + P:SEQ + 2 * P].rearrange("p a k -> p (a k)"))
                    gp.tensor_copy(vsmp[:, :], V[:, NT, bass.ds(i * P, P)])
                gp.tensor_copy(vst[:, par, :, :], V[:, t:t + 2, bass.ds(i * P, P)]).then_inc(staged, 1)

            def q_rms(i, t):
                par, q = t % 2, STEPS * i + t
                gp.wait_ge(s0_used, q + 1)
                gp.tensor_tensor(rs[:, par, :], ms[:, par, :], neghalf[:, :], ALU.pow).then_inc(rs_ready, 1)

            gp.wait_ge(consts_made, 10)
            gp.wait_ge(bank_free[2], 12)
            gp.wait_ge(kq_done, 1)
            with gp.Fori(0, 2) as i:
                stage(i, 0)
                q_rms(i, 0)
                for t in range(STEPS):
                    split_lo(Slab(PAIR_SLAB + t + 1, 10, i))
                    if t + 1 < STEPS:
                        stage(i, t + 1)
                        q_rms(i, t + 1)
                for jj in range(2):
                    split_lo(Slab(PAIR_SLAB + 9 + jj, 10, i))
            with gp.Fori(2, 4) as i:
                for c in range(10):
                    split_lo(Slab(PAIR_SLAB + c + 1, 10, i))
            gp.wait_ge(tout_done, 2)
            gp.dma_start(io["new_conv_prompt"][0, 0], tout[0:2, :]).then_inc(small_out, 16)
            gp.dma_start(io["new_conv_sample"][0].rearrange("b r c -> (b r) c"), tout[2:2 + 2 * DEC_B, :])\
                .then_inc(small_out, 16)
            for n in range(OUT_SLAB + 1, FFN_SLAB + 4 + 1):
                split_lo(Slab(n))
            with gp.Fori(0, (NCH - 1) // 2) as i:
                for c in range(12):
                    split_lo(Slab(FFN_SLAB + 5 + c, 12, i))
            split_lo(Slab(FFN_SLAB + 65))
            gp.wait_ge(small_out, 96)

        @block.scalar
        def _(act):
            def split_hi(slab, *free):
                act.wait_ge(raw_in[slab.slot], 32 * (slab.turn + 1))
                if free:
                    slab_is_done(act, *free)
                act.activation(ws[slab.slot][0][:, :], raw[slab.slot][:, :], ACT.Copy).then_inc(w_hi, 1)

            def norm_stats(ph, t):
                if ph == 0:
                    act.wait_ge(x_in[t], 16)
                else:
                    act.wait_ge(d_free, 7 * NT + t + 1)
                q = (NT + 6) * ph + t
                if q:
                    act.wait_ge(sq_done, q)
                scratch = (scratch_p, scratch_f)[ph]
                act.activation(scratch[:, :], X[:, t, :], ACT.Square, accum_out=ss[:, t:t + 1]).then_inc(sq_done, 1)
                act.wait_ge(sq_done, q + 1)
                act.activation(sd[:, t:t + 1], ss[:, t:t + 1], ACT.Sqrt, bias=eps[:, :], scale=1.0 / D).then_inc(sd_done, 1)

            def norm_hi_part(ph, t):
                for h in range(2):
                    idx = 2 * (NT * ph + t) + h
                    act.wait_ge(nT_done, idx + 1)
                    src = banks[:, (2 * t + h) % 3, :].rearrange("p (k c) -> p k c", k=4)
                    act.activation(xs[0][:, 4 * h:4 * h + 4, t * P:(t + 1) * P], src, ACT.Copy).then_inc(norm_hi, 1)

            act.wait_ge(consts_made, 10)
            norm_stats(0, 0)
            split_hi(Slab(0))
            norm_stats(0, 1)

            def v_evac(a, g):
                w = 3 * a + g
                act.wait_ge(gemm_ready, w + 1)
                if w >= 2:
                    act.wait_ge(vt_ready, w - 1)
                act.activation(S[:, w % 2, :], banks[:, g, 0:G], ACT.Copy).then_inc(bank_free[g], 1)

            for g in range(NG):
                for t in range(3 * g, 3 * g + 3):
                    norm_hi_part(0, t)
                    if t + 2 < NT:
                        norm_stats(0, t + 2)
                if g == 0:
                    split_hi(Slab(1))
                v_evac(0, g)
            split_hi(Slab(2), "f", 0)
            for g in range(NG):
                v_evac(1, g)
            split_hi(Slab(3), "f", 1)

            def k_root(w):
                act.wait_ge(k_ms, w + 1)
                if w >= 3:
                    act.wait_ge(bank_free[w % 3], 3 - (w < 3))
                act.activation(kr[:, w % 3, :], banks[:, 3 + w % 2, 0:G], ACT.Sqrt, bias=eps[:, :],
                               scale=1.0 / HD).then_inc(k_sd, 1)

            for w in range(6):
                g = w % 3
                act.wait_ge(gemm_ready, 6 + w + 1)
                if w >= 2:
                    act.wait_ge(k_ms, w - 1)
                else:
                    act.wait_ge(vt_ready, 6)
                act.activation(S[:, w % 2, :], banks[:, g, 0:G], ACT.Square).then_inc(sq_done, 1)
                k_root(w)
                if w == 2:
                    split_hi(Slab(4), "f", 2)

            with act.Fori(0, 2) as i:
                for j in range(4):
                    split_hi(Slab(Q_SLAB + j + 1, 4, i), "f", Q_SLAB + 4 * i + j - 1)
                    for g in range(NG):
                        act.wait_ge(gemm_ready, 3 * (Q_SLAB + 4 * i + j) + g + 1)
                        act.activation(O[:, bass.ds(4 * i + j, 1), g * G:(g + 1) * G].rearrange("p a c -> p (a c)"),
                                       banks[:, g, 0:G], ACT.Copy).then_inc(bank_free[g], 1)

            def out_transposed(i, t, u):
                z = SLOTS * i + 3 * t + u
                act.wait_ge(s2_done, z + 1)
                n = 4 * P if u < 2 else P
                act.activation(PT[:, 1, :, :].rearrange("p h q -> p (h q)")[:, 0:n], banks[:, 6, 0:n], ACT.Copy)\
                    .then_inc(pt_a, 1)

            def out_attention(i, t, u):
                z = SLOTS * i + 3 * t + u
                act.wait_ge(s3_done, z + 1)
                if u < 2:
                    dst = O[:, bass.ds(4 * i + 2 * u, 2), t * P:(t + 1) * P]
                    src = banks[:, 7, 0:2 * P].rearrange("p (b q) -> p b q", b=2)
                else:
                    dst = O[:, bass.ds(4 * i, 4), SEQ + t * DEC_T:SEQ + (t + 1) * DEC_T]
                    src = banks[:, 7, 0:4 * DEC_T].rearrange("p (b q) -> p b q", b=4)
                act.activation(dst, src, ACT.Copy, scale=0.5).then_inc(o_done, 1)

            def exps(i, t, u):
                z, par = SLOTS * i + 3 * t + u, t % 2
                act.wait_ge(soft_done, 7 * z + 5)
                for h in range(4 if u < 2 else 1):
                    scale = rs[:, par, 2 * h + u:2 * h + u + 1] if u < 2 else rs[:, par, 8:9]
                    act.activation(Pb[:, h, :], scores[:, h, :], ACT.Exp, bias=soft[:, 3, h:h + 1], scale=scale,
                                   accum_out=soft[:, 5, h:h + 1])
                n = 4 if u < 2 else 1
                act.activation(soft[:, 6, 0:n], soft[:, 4, 0:n], ACT.Exp).then_inc(exp_done, 1)

            def unit(i, c, g):
                f = PAIR_SLAB + 10 * i + c
                bank = banks[:, g, 0:G]
                jj, kind = (c // 4, c % 4) if c < 8 else (c - 8, 4)
                if kind == 0:
                    act.wait_ge(gemm_ready, 3 * f + g + 1)
                    act.wait_ge(merged, 6 * i + 1)
                    act.activation(A[:, jj, g * G:(g + 1) * G], bank, ACT.Copy).then_inc(bank_free[g], 1)
                elif kind >= 3:
                    e = 12 * i + (3 * jj if kind == 3 else 6 + 3 * jj) + g
                    act.wait_ge(gemm_ready, 3 * f + g + 1)
                    slot = (3 * jj + g) % 2
                    if c > 3 or g > 1:
                        act.wait_ge(sg_used, e - 1)
                    act.activation(S[:, slot, :], bank, ACT.Tanh, scale=0.5).then_inc(bank_free[g], 1)

            with act.Fori(0, 2) as i:
                for t in range(STEPS):
                    split_hi(Slab(PAIR_SLAB + t + 1, 10, i), "f", PAIR_SLAB + 10 * i + t - 1)
                    for u in range(3):
                        if 3 * t + u:
                            before = ((t, u - 1) if u else (t - 1, 2))
                            out_transposed(i, *before)
                            out_attention(i, *before)
                        exps(i, t, u)
                        unit(i, t, u)
                split_hi(Slab(PAIR_SLAB + 9, 10, i), "f", PAIR_SLAB + 10 * i + 7)
                out_transposed(i, STEPS - 1, 2)
                out_attention(i, STEPS - 1, 2)
                for g in range(NG):
                    unit(i, 8, g)
                split_hi(Slab(PAIR_SLAB + 10, 10, i), "f", PAIR_SLAB + 10 * i + 8)
                for g in range(NG):
                    unit(i, 9, g)
            with act.Fori(2, 4) as i:
                for c in range(10):
                    split_hi(Slab(PAIR_SLAB + c + 1, 10, i), "f", PAIR_SLAB + 10 * i + c - 1)
                    for g in range(NG):
                        unit(i, c, g)

            def merged_hi(c):
                act.wait_ge(merged, 1 + (6 * (c + 1) if c != 1 else 24))
                if c == 1:
                    act.wait_ge(small_out, 96)
                if c >= 2:
                    slab_is_done(act, "d", 2 * (c - 2) + 1)
                act.activation(acts[c % 2][:, :, 0, :], O[:, 2 * c:2 * c + 2, :], ACT.Copy).then_inc(m_hi, 1)

            merged_hi(0)
            for c in range(4):
                for hf in range(2):
                    s = 2 * c + hf
                    free = ("d", s - 1) if s else ("f", OUT_SLAB - 1)
                    split_hi(Slab(OUT_SLAB + s + 1), *free)
                    if hf == 0 and c < 3:
                        merged_hi(c + 1)

            def gate(first, per, i, b, g):
                f = first + per * i
                act.wait_ge(gemm_ready, 3 * f + g + 1)
                act.activation(Gt[:, b, g * G:(g + 1) * G], banks[:, g, 0:G], ACT.Silu).then_inc(bank_free[g], 1)

            def up(first, per, i, slot, b, g):
                f = first + per * i
                act.wait_ge(bank_free[g], f + 1)
                act.activation(acts[slot][:, b, 0, g * G:(g + 1) * G], Ht[:, (3 * b + g) % 2, :], ACT.Copy)\
                    .then_inc(f_hi, 1)

            F0 = OUT_SLAB
            act.wait_ge(m_lo, 4)
            norm_stats(1, 0)
            norm_stats(1, 1)
            for g in range(NG):
                for t in range(3 * g, 3 * g + 3):
                    norm_hi_part(1, t)
                    if t + 2 < NT:
                        norm_stats(1, t + 2)
                if g == 0:
                    split_hi(Slab(FFN_SLAB + 1), "d", 7)
                gate(F0, 0, 0, 0, g)
            split_hi(Slab(FFN_SLAB + 2), "f", F0)
            for g in range(NG):
                up(F0 + 1, 0, 0, 0, 0, g)
            split_hi(Slab(FFN_SLAB + 3), "f", F0 + 1)
            for g in range(NG):
                gate(F0 + 2, 0, 0, 1, g)
            split_hi(Slab(FFN_SLAB + 4), "f", F0 + 2)
            for g in range(NG):
                up(F0 + 3, 0, 0, 0, 1, g)

            with act.Fori(0, (NCH - 1) // 2) as i:
                for odd in range(2):
                    n0 = FFN_SLAB + 4 + 6 * odd
                    f0 = F0 + 4 + 4 * odd
                    s0 = 8 + 2 * odd
                    slot = 1 - odd
                    for b in range(2):
                        for k in range(2):
                            idx = 2 * b + k
                            if idx == 0:
                                if odd:
                                    free = ("d", s0 - 2 + 4 * i + 1)
                                else:
                                    free = None
                            else:
                                free = ("f", f0 + idx - 1 + 8 * i)
                            if free is None:
                                act.wait_ge(gemm_ready, 3 * (F0 + 4 + 8 * i))
                                act.wait_ge(d_ready, NT * (8 + 4 * i))
                                split_hi(Slab(n0 + 1, 12, i))
                            else:
                                split_hi(Slab(n0 + idx + 1, 12, i), *free)
                            for g in range(NG):
                                if k == 0:
                                    gate(f0 + idx, 8, i, b, g)
                                else:
                                    up(f0 + idx, 8, i, slot, b, g)
                    split_hi(Slab(n0 + 5, 12, i), "f", f0 + 3 + 8 * i)
                    split_hi(Slab(n0 + 6, 12, i), "d", s0 + 4 * i)
            split_hi(Slab(FFN_SLAB + 65), "d", 8 + 2 * (NCH - 1) - 1)

        @block.vector
        def _(dve):
            def norm_scale(ph, t):
                xn, wbc = ((xn_p, wbc_p), (xn_f, wbc_f))[ph]
                q = NT * ph + t
                dve.wait_ge(sd_done, q + 1)
                dve.reciprocal(rms[:, t:t + 1], sd[:, t:t + 1]).then_inc(rms_done, 1)
                if t >= 2:
                    dve.wait_ge(nT_done, 2 * (q - 1))
                dve.wait_ge(rms_done, q + 1)
                dve.scalar_tensor_tensor(out=xn[:, t % 2, :], in0=X[:, t, :], scalar=rms[:, t:t + 1], in1=wbc[:, :],
                                         op0=ALU.mult, op1=ALU.mult).then_inc(xn_ready, 1)

            def norm_lo_part(ph, t):
                for h in range(2):
                    idx = 2 * (NT * ph + t) + h
                    dve.wait_ge(norm_hi, idx + 1)
                    src = banks[:, (2 * t + h) % 3, :].rearrange("p (k c) -> p k c", k=4)
                    where = (slice(None), slice(4 * h, 4 * h + 4), slice(t * P, (t + 1) * P))
                    dve.tensor_tensor(xs[1][where], src, xs[0][where].bitcast(F32), ALU.subtract).then_inc(norm_lo, 1)

            dve.wait_ge(const_in, 16 * 15)
            dve.wait_ge(wbc_in, 16)
            norm_scale(0, 0)
            dve.wait_ge(smallT, 2)
            dve.tensor_copy(stT[:, :, :, :].rearrange("p b r j -> p (b r j)"), banks[:, 5, 0:P]).then_inc(small_done, 1)
            dve.tensor_scalar(cwT[:, :, :].rearrange("p w j -> p (w j)"), banks[:, 5, P:P + 24], 0.5, None, ALU.mult)\
                .then_inc(small_done, 1)
            norm_scale(0, 1)

            def v_rows(w):
                a, g = divmod(w, 3)
                dve.wait_ge(vt_ready, w + 1)
                dve.tensor_copy(V[:, 1 + 3 * g:4 + 3 * g, a * P:(a + 1) * P],
                                banks[:, 3 + w % 2, 0:G].rearrange("p (t c) -> p t c", t=3)).then_inc(v_done, 1)

            for g in range(NG):
                for t in range(3 * g, 3 * g + 3):
                    norm_lo_part(0, t)
                    if t + 2 < NT:
                        norm_scale(0, t + 2)
            for w in range(6):
                v_rows(w)
            for w in range(6):
                a, g = divmod(w, 3)
                dve.wait_ge(k_sd, w + 1)
                dve.reciprocal(kr[:, w % 3, :], kr[:, w % 3, :]).then_inc(k_rs, 1)
                dve.wait_ge(k_rs, w + 1)
                dve.scalar_tensor_tensor(out=kT[:, a, P + g * G:P + (g + 1) * G], in0=banks[:, g, 0:G], scalar=knw[:, :],
                                         in1=kr[:, w % 3, :], op0=ALU.mult, op1=ALU.mult).then_inc(bank_free[g], 1)
            dve.wait_ge(kt_ready, 1)
            dve.tensor_copy(kout[:, :, :].rearrange("p t c -> p (t c)"), banks[:, 3, :]).then_inc(kout_done, 1)
            dve.wait_ge(bank_free[2], 4)
            dve.wait_ge(pads_done, 3)
            dve.tensor_scalar(kT[:, :, :], kT[:, :, :], qnw[:, :], None, ALU.mult).then_inc(kq_done, 1)

            def after_s0(i, t):
                q, par = STEPS * i + t, t % 2
                dve.wait_ge(s0_done, q + 1)
                dve.tensor_scalar(ms[:, par, :], banks[:, 7, 0:9], HD * EPS, None, ALU.add)
                dve.tensor_scalar(ks[:, par, :], banks[:, 7, P:2 * P], qnw[:, :], None, ALU.mult).then_inc(s0_used, 1)

            def out_transposed(i, t, u):
                z = SLOTS * i + 3 * t + u
                dve.wait_ge(s2_done, z + 1)
                n = 4 * P if u < 2 else P
                dve.tensor_copy(PT[:, 0, :, :].rearrange("p h q -> p (h q)")[:, 0:n], banks[:, 5, 0:n]).then_inc(pt_v, 1)

            def softmax_bias(i, t, u):
                z, par = SLOTS * i + 3 * t + u, t % 2
                n = 4 if u < 2 else 1
                r = rs[:, par, u:u + 7:2] if u < 2 else rs[:, par, 8:9]
                sink = sinkb[:, bass.ds(8 * i + 4 * u, 4)] if u < 2 else sinkS[:, bass.ds(i, 1)]
                dve.wait_ge(s1_done, z + 1)
                dve.tensor_reduce(soft[:, 0, 0:n], scores[:, 0:n, :], AX_X, ALU.max).then_inc(soft_done, 1)
                dve.wait_ge(rs_ready, STEPS * i + t + 1)
                dve.wait_ge(soft_done, 7 * z + 1)
                dve.tensor_tensor(soft[:, 1, 0:n], soft[:, 0, 0:n], r, ALU.mult).then_inc(soft_done, 1)
                dve.wait_ge(soft_done, 7 * z + 2)
                dve.tensor_tensor(soft[:, 2, 0:n], soft[:, 1, 0:n], sink, ALU.max).then_inc(soft_done, 1)
                dve.wait_ge(soft_done, 7 * z + 3)
                dve.tensor_scalar(soft[:, 3, 0:n], soft[:, 2, 0:n], -1.0, None, ALU.mult).then_inc(soft_done, 1)
                dve.wait_ge(soft_done, 7 * z + 4)
                dve.tensor_tensor(soft[:, 4, 0:n], soft[:, 3, 0:n], sink, ALU.add).then_inc(soft_done, 1)

            def normalise(i, t, u):
                z = SLOTS * i + 3 * t + u
                n = 4 if u < 2 else 1
                dve.wait_ge(exp_done, z + 1)
                dve.tensor_tensor(soft[:, 7, 0:n], soft[:, 5, 0:n], soft[:, 6, 0:n], ALU.add).then_inc(soft_done, 1)
                dve.wait_ge(soft_done, 7 * z + 6)
                dve.reciprocal(soft[:, 8, 0:n], soft[:, 7, 0:n]).then_inc(soft_done, 1)
                dve.wait_ge(soft_done, 7 * z + 7)
                for h in range(n):
                    ins = dve.tensor_scalar(Pb[:, h, :], Pb[:, h, :], soft[:, 8, h:h + 1], None, ALU.mult)
                ins.then_inc(p_ready, 1)

            def u_parts(g):
                lo, hi = g * G, min((g + 1) * G, SEQ)
                return lo, hi

            def sample_view(buf, off):
                return buf[:, UP0:UW].rearrange("p (b c) -> p b c", b=DEC_B)[:, :, off:off + DEC_T]

            def sample_cols(a):
                return a[:, SEQ:TOK].rearrange("p (b c) -> p b c", b=DEC_B)

            def conv(i, jj, g):
                lo, hi = u_parts(g)
                base = 18 * i + 3 * (3 * jj + g)
                dve.wait_ge(bank_free[g], PAIR_SLAB + 10 * i + 4 * jj + 2)
                for k in range(3):
                    w = cwT[:, k, bass.ds(2 * i + jj, 1)]
                    if k:
                        dve.wait_ge(conv_step, base + k)
                    parts = [(A[:, jj, lo:hi], U[:, lo + k:hi + k])]
                    if g == 2:
                        parts.append((sample_cols(A[:, jj, :]), sample_view(U, k)))
                    for y, src in parts:
                        if k == 0:
                            ins = dve.tensor_scalar(y, src, w, None, ALU.mult)
                        else:
                            ins = dve.scalar_tensor_tensor(out=y, in0=src, scalar=w, in1=y, op0=ALU.mult, op1=ALU.add)
                    ins.then_inc(conv_step, 1)
                if g == 2:
                    j = bass.ds(2 * i + jj, 1)
                    dve.tensor_copy(tails[:, j, 0:2].rearrange("p a r -> p (a r)"), U[:, UP0 - 2:UP0])
                    dve.tensor_copy(tails[:, j, 2:].rearrange("p a (b r) -> p (a b) r", r=2),
                                    sample_view(U, 2)[:, :, DEC_T - 2:DEC_T]).then_inc(tail_step, 1)

            def unit(i, c, g):
                f = PAIR_SLAB + 10 * i + c
                bank = banks[:, g, 0:G]
                jj, kind = (c // 4, c % 4) if c < 8 else (c - 8, 4)
                a = A[:, jj, g * G:(g + 1) * G]
                if kind == 1:
                    lo, hi = u_parts(g)
                    if g == 0:
                        dve.tensor_copy(U[:, UP0:UW].rearrange("p (b c) -> p b c", b=DEC_B)[:, :, 0:2],
                                        stT[:, :, :, bass.ds(2 * i + jj, 1)].rearrange("p b r a -> p b (r a)"))
                    dve.wait_ge(gemm_ready, 3 * f + g + 1)
                    dve.wait_ge(bank_free[g], f)
                    ins = dve.tensor_tensor(U[:, 2 + lo:2 + hi], bank[:, 0:hi - lo], A[:, jj, lo:hi], ALU.mult)
                    if g == 2:
                        ins = dve.tensor_tensor(sample_view(U, 2),
                                                bank[:, hi - lo:G].rearrange("p (b c) -> p b c", b=DEC_B),
                                                sample_cols(A[:, jj, :]), ALU.mult)
                    ins.then_inc(bank_free[g], 1)
                elif kind == 2:
                    dve.wait_ge(gemm_ready, 3 * f + g + 1)
                    dve.wait_ge(conv_step, 18 * i + 9 * (jj + 1))
                    dve.tensor_tensor(a, bank, a, ALU.mult).then_inc(bank_free[g], 1)
                elif kind == 3:
                    dve.wait_ge(bank_free[g], f + 1)
                    dve.scalar_tensor_tensor(out=a, in0=S[:, (3 * jj + g) % 2, :], scalar=1.0, in1=a, op0=ALU.add,
                                             op1=ALU.mult).then_inc(sg_used, 1)
                elif kind == 4:
                    o = O[:, bass.ds(2 * i + jj, 1), g * G:(g + 1) * G].rearrange("p a c -> p (a c)")
                    e = 12 * i + 6 + 3 * jj + g
                    dve.wait_ge(bank_free[g], f + 1)
                    dve.wait_ge(o_done, SLOTS * min2(i))
                    dve.scalar_tensor_tensor(out=o, in0=S[:, (3 * jj + g) % 2, :], scalar=1.0, in1=o, op0=ALU.add,
                                             op1=ALU.mult).then_inc(sg_used, 1)
                    dve.wait_ge(sg_used, e + 1)
                    dve.tensor_tensor(o, o, a, ALU.add).then_inc(merged, 1)

            attention_on = [True]

            def min2(i):
                return i + 1 if attention_on[0] else 2

            dve.wait_ge(small_done, 2)
            dve.memset(U[:, 0:2], 0.0).then_inc(merged, 1)
            with dve.Fori(0, 2) as i:
                after_s0(i, 0)
                for t in range(STEPS):
                    for u in range(3):
                        if 3 * t + u:
                            bt, bu = (t, u - 1) if u else (t - 1, 2)
                            out_transposed(i, bt, bu)
                            if bt % 4 == 1:
                                conv(i, bt // 4, bu)
                            if bu == 1 and bt + 1 < STEPS:
                                after_s0(i, bt + 1)
                        softmax_bias(i, t, u)
                        normalise(i, t, u)
                        unit(i, t, u)
                out_transposed(i, STEPS - 1, 2)
                for jj in range(2):
                    for g in range(NG):
                        unit(i, 8 + jj, g)
            attention_on[0] = False
            with dve.Fori(2, 4) as i:
                for c in range(10):
                    for g in range(NG):
                        unit(i, c, g)
                        if c % 4 == 1 and c < 8:
                            conv(i, c // 4, g)

            def merged_lo(c):
                dve.wait_ge(m_hi, c + 1)
                dve.tensor_tensor(acts[c % 2][:, :, 1, :], O[:, 2 * c:2 * c + 2, :],
                                  acts[c % 2][:, :, 0, :].bitcast(F32), ALU.subtract).then_inc(m_lo, 1)

            def add_rows(s, hf, x_turn=None):
                for t in range(NT):
                    x = X[:, t, hf * 512:(hf + 1) * 512]
                    dve.wait_ge(d_ready, NT * s + t + 1)
                    if x_turn is not None:
                        dve.wait_ge(x_in[t], x_turn)
                    else:
                        dve.wait_ge(d_free, NT * (s - 2) + t + 1)
                    dve.tensor_tensor(x, banks[:, 3 + t % DU, :], x, ALU.add).then_inc(d_free, 1)

            merged_lo(0)
            dve.wait_ge(tailsT, 2)
            for h in range(2):
                dve.tensor_copy(tout[:, h * 512:(h + 1) * 512], banks[0:2 + 2 * DEC_B, 3 + h, :]).then_inc(tout_done, 1)
            for c in range(4):
                add_rows(2 * c, 0, 32 if c == 0 else None)
                if c < 3:
                    merged_lo(c + 1)
                if c < 3:
                    add_rows(2 * c + 1, 1, 32 if c == 0 else None)

            dve.wait_ge(wbc_in, 32)
            for t in range(NT):
                x = X[:, t, 512:D]
                dve.wait_ge(d_ready, NT * 7 + t + 1)
                dve.wait_ge(d_free, NT * 5 + t + 1)
                dve.tensor_tensor(x, banks[:, 3 + t % DU, :], x, ALU.add).then_inc(d_free, 1)
                if t == 2:
                    norm_scale(1, 0)
                if t == 4:
                    norm_scale(1, 1)
            for t in range(NT):
                norm_lo_part(1, t)
                if t + 2 < NT:
                    norm_scale(1, t + 2)

            def up(first, per, i, c, slot, b, g):
                f = first + per * i
                fu = 6 * c + 3 * b + g
                h = Ht[:, (3 * b + g) % 2, :]
                dve.wait_ge(gemm_ready, 3 * f + g + 1)
                dve.wait_ge(bank_free[g], f)
                if not isinstance(fu, int) or fu >= 2:
                    dve.wait_ge(f_lo, fu - 1)
                dve.tensor_tensor(h, banks[:, g, 0:G], Gt[:, b, g * G:(g + 1) * G], ALU.mult).then_inc(bank_free[g], 1)
                dve.wait_ge(f_hi, fu + 1)
                dve.tensor_tensor(acts[slot][:, b, 1, g * G:(g + 1) * G], h,
                                  acts[slot][:, b, 0, g * G:(g + 1) * G].bitcast(F32), ALU.subtract).then_inc(f_lo, 1)

            F0 = OUT_SLAB
            for b in range(2):
                for g in range(NG):
                    up(F0 + 2 * b + 1, 0, 0, 0, 0, b, g)
            with dve.Fori(0, (NCH - 1) // 2) as i:
                for odd in range(2):
                    for b in range(2):
                        for g in range(NG):
                            up(F0 + 4 + 4 * odd + 2 * b + 1, 8, i, 2 * i + 1 + odd, 1 - odd, b, g)
                    for hf in range(2):
                        add_rows(8 + 4 * i + 2 * odd + hf, hf)
            for hf in range(2):
                add_rows(8 + 2 * (NCH - 1) + hf, hf)

        @block.tensor
        def _(pe):
            def feature_unit(slot, f, g, hook=None):
                if not isinstance(f, int) or f > 0:
                    pe.wait_ge(bank_free[g], f)
                for kt in range(KT):
                    if kt == 2 and hook is not None:
                        hook()
                    for n, (w, x) in enumerate(PASSES):
                        mm = pe.matmul(banks[:, g, 0:G], ws[slot][w][:, kt * P:(kt + 1) * P],
                                       xs[x][:, kt, g * G:(g + 1) * G],
                                       start=(kt == 0 and n == 0), stop=(kt == KT - 1 and n == 2))
                mm.then_inc(gemm_ready, 1)

            def norm_transpose(ph, t):
                xn = (xn_p, xn_f)[ph]
                pe.wait_ge(xn_ready, NT * ph + t + 1)
                for h in range(2):
                    idx = 2 * t + h
                    if idx >= 3:
                        pe.wait_ge(norm_lo, 2 * NT * ph + idx - 2)
                    for k in range(4):
                        kt = 4 * h + k
                        mm = pe.transpose(banks[:, idx % 3, k * P:(k + 1) * P], xn[:, t % 2, kt * P:(kt + 1) * P],
                                          ident[:, :])
                    mm.then_inc(nT_done, 1)

            def normed_slab(ph, slot, f, hook=lambda g: None):
                for g in range(NG):
                    if g:
                        pe.wait_ge(bank_free[g - 1], f + 1)
                    for t in range(3 * g, 3 * g + 3):
                        norm_transpose(ph, t)
                    pe.wait_ge(norm_lo, 2 * NT * ph + 6 * (g + 1))
                    feature_unit(slot, f, g, hook(g))

            pe.wait_ge(const_in, 16 * 15)
            pe.wait_ge(consts_made, 10)
            pe.transpose(banks[:, 5, 0:P], rows_st, ident[:, :]).then_inc(smallT, 1)
            pe.transpose(banks[:, 5, P:P + 24], rows_cw, ident[0:24, 0:24]).then_inc(smallT, 1)

            def v_transpose(w):
                pe.wait_ge(bank_free[w % 3], w // 3 + 1)
                if w >= 2:
                    pe.wait_ge(v_done, w - 1)
                for t in range(3):
                    mm = pe.transpose(banks[:, 3 + w % 2, t * P:(t + 1) * P], S[:, w % 2, t * P:(t + 1) * P], ident[:, :])
                mm.then_inc(vt_ready, 1)

            def k_mean_square(w):
                pe.wait_ge(sq_done, NT + w + 1)
                if w < 2:
                    pe.wait_ge(v_done, 6)
                else:
                    pe.wait_ge(k_sd, w - 1)
                pe.matmul(banks[:, 3 + w % 2, 0:G], blockones[:, :], S[:, w % 2, :], start=True, stop=True)\
                    .then_inc(k_ms, 1)

            pe.wait_ge(w_lo, 1)
            normed_slab(0, 0, 0, lambda g: (lambda: v_transpose(g - 1)) if g else None)
            pe.wait_ge(w_lo, 2)
            for g in range(NG):
                feature_unit(1, 1, g, lambda: v_transpose(2 + g))
            for a in range(2):
                pe.wait_ge(w_lo, 3 + a)
                for g in range(NG):
                    w = 3 * a + g
                    feature_unit(a, 2 + a, g, (lambda: k_mean_square(w - 1)) if w else (lambda: v_transpose(5)))
            k_mean_square(5)

            with pe.Fori(0, 2) as i:
                for j in range(4):
                    n = Q_SLAB + 4 * i + j
                    pe.wait_ge(w_lo, n + 1)
                    for g in range(NG):
                        feature_unit(j % 2, n, g)

            pe.wait_ge(bank_free[2], 4)
            for t in range(2):
                for a in range(2):
                    mm = pe.transpose(banks[:, 3, (2 * t + a) * P:(2 * t + a + 1) * P],
                                      kT[:, a, (NT - 1 + t) * P:(NT + t) * P], ident[:, :])
            mm.then_inc(kt_ready, 1)

            def s0(i, t):
                q, par = STEPS * i + t, t % 2
                pe.wait_ge(staged, q + 1)
                pe.wait_ge(cache_in[par], 32 * (4 * i + t // 2 + 1))
                if t:
                    pe.wait_ge(o_done, SLOTS * i + 3 * (t - 1) + 1)
                for h in range(4):
                    pe.matmul(banks[:, 7, 2 * h:2 * h + 2], sqst[:, h, :], ones2[:, :], start=True, stop=True)
                for s in range(2):
                    half = slice(HD * s, HD * (s + 1))
                    pe.matmul(banks[half, 7, 8:9], sqs[half, :, :].rearrange("p h c -> p (h c)"), ones2[half, s:s + 1],
                              start=True, stop=True)
                pe.transpose(banks[:, 7, P:2 * P], ck[:, par, :], ident[:, :]).then_inc(s0_done, 1)

            def s1(i, t, u):
                z, par = SLOTS * i + 3 * t + u, t % 2
                if u < 2:
                    half = slice(HD * u, HD * (u + 1))
                    variant = 1 if t else 0
                    for b in range(2):
                        for h in range(2):
                            pe.matmul(scores[:, 2 * b + h, :], halves[:, :], mask[:, variant, :], start=(h == 0),
                                      stop=False, skip_group_check=True)
                        for h in range(2):
                            mm = pe.matmul(scores[:, 2 * b + h, :], qst[half, par, 2 * b + h, :], kst[half, par, :],
                                           start=False, stop=(h == 1), skip_group_check=True)
                else:
                    pe.wait_ge(s0_used, STEPS * i + t + 1)
                    off = P - DEC_T - DEC_T * t
                    pe.matmul(scores[:, 0, P:2 * P], ones_row[:, :], window[:, off:off + P], start=True, stop=False,
                              skip_group_check=True)
                    for s in range(2):
                        half = slice(HD * s, HD * (s + 1))
                        for k, keys in enumerate((ks[half, par, :], ksmp[half, :])):
                            mm = pe.matmul(scores[half, 0, k * P:(k + 1) * P],
                                           qs[half, par, :, :].rearrange("p h c -> p (h c)"), keys,
                                           start=False, stop=(k == 1), skip_group_check=True)
                mm.then_inc(s1_done, 1)

            def s2(i, t, u):
                z = SLOTS * i + 3 * t + u
                pe.wait_ge(p_ready, z + 1)
                for k in range(2):
                    for h in range(4 if u < 2 else 1):
                        mm = pe.transpose(banks[:, 5 + k, h * P:(h + 1) * P], Pb[:, h, k * P:(k + 1) * P], ident[:, :])
                mm.then_inc(s2_done, 1)

            def s3(i, t, u, s0_before=None):
                z, par = SLOTS * i + 3 * t + u, t % 2
                pe.wait_ge(pt_v, z + 1)
                pe.wait_ge(pt_a, z + 1)
                if 3 * t + u:
                    pe.wait_ge(o_done, z)
                if s0_before is not None:
                    pe.wait_ge(s0_used, STEPS * i + s0_before + 1)
                for e in range(2):
                    half = slice(HD * e, HD * (e + 1))
                    if u < 2:
                        out = banks[half, 7, 0:2 * P]
                        for k in range(2):
                            mm = pe.matmul(out, vst[:, par, k, HD * u:HD * (u + 1)], PT[:, k, e:e + 3:2, :],
                                           start=(k == 0), stop=(k == 1))
                    else:
                        for s in range(2):
                            out = banks[half, 7, 2 * DEC_T * s:2 * DEC_T * (s + 1)]
                            for k, v in enumerate((cv[:, par, :], vsmp[:, :])):
                                rows = PT[:, k, 0, :].rearrange("p (s h c) -> p s h c", s=2, h=4)[:, s, e:e + 3:2, :]
                                mm = pe.matmul(out, v[:, HD * s:HD * (s + 1)], rows, start=(k == 0), stop=(k == 1))
                mm.then_inc(s3_done, 1)

            pe.wait_ge(masks_done, 11)
            with pe.Fori(0, 2) as i:
                s0(i, 0)
                for t in range(STEPS):
                    f = PAIR_SLAB + 10 * i + t
                    for u in range(3):
                        if 3 * t + u:
                            bt, bu = (t, u - 1) if u else (t - 1, 2)
                            s2(i, bt, bu)
                        s1(i, t, u)
                        if 3 * t + u:
                            s3(i, bt, bu, (t + 1 if t + 1 < STEPS else None) if u == 2 else (0 if t == 0 and u == 1 else None))
                        if u == 0:
                            pe.wait_ge(w_lo, f + 1)
                        feature_unit(t % 2, f, u)
                        if u == 1 and t + 1 < STEPS:
                            s0(i, t + 1)
                s2(i, STEPS - 1, 2)
                for jj in range(2):
                    f = PAIR_SLAB + 10 * i + 8 + jj
                    pe.wait_ge(w_lo, f + 1)
                    for g in range(NG):
                        feature_unit(jj, f, g, (lambda: s3(i, STEPS - 1, 2)) if jj == 0 and g == 0 else None)
            with pe.Fori(2, 4) as i:
                for c in range(10):
                    f = PAIR_SLAB + 10 * i + c
                    pe.wait_ge(w_lo, f + 1)
                    for g in range(NG):
                        feature_unit(c % 2, f, g)

            pe.wait_ge(tail_step, 8)
            for h in range(2):
                for k in range(4):
                    mm = pe.transpose(banks[0:2 + 2 * DEC_B, 3 + h, k * P:(k + 1) * P], tails[:, 4 * h + k, :], ident[:, :])
                mm.then_inc(tailsT, 1)

            def row_units(slot, s, hf, act_slot, first=False):
                for t in range(NT):
                    bank = 3 + t % DU
                    if t >= DU:
                        pe.wait_ge(d_free, NT * s + t - DU + 1)
                    elif not first:
                        pe.wait_ge(d_free, NT * (s - 1) + t + (DU if t + DU < NT else 0) + 1)
                    for k in range(2):
                        for n, (w, x) in enumerate(PASSES):
                            mm = pe.matmul(banks[:, bank, :], acts[act_slot][:, k, x, t * P:(t + 1) * P],
                                           ws[slot][w][:, k * 512:(k + 1) * 512],
                                           start=(k == 0 and n == 0), stop=(k == 1 and n == 2))
                    mm.then_inc(d_ready, 1)

            for c in range(4):
                pe.wait_ge(m_lo, c + 1)
                if c == 0:
                    pe.wait_ge(tout_done, 2)
                for hf in range(2):
                    pe.wait_ge(w_lo, OUT_SLAB + 2 * c + hf + 1)
                    row_units(hf, 2 * c + hf, hf, c % 2, first=(c == 0 and hf == 0))

            F0 = OUT_SLAB
            pe.wait_ge(w_lo, FFN_SLAB + 1)
            normed_slab(1, 0, F0)
            for k in range(1, 4):
                pe.wait_ge(w_lo, FFN_SLAB + k + 1)
                for g in range(NG):
                    feature_unit(k % 2, F0 + k, g)
            with pe.Fori(0, (NCH - 1) // 2) as i:
                for odd in range(2):
                    n0 = FFN_SLAB + 4 + 6 * odd + 12 * i
                    f0 = F0 + 4 + 4 * odd + 8 * i
                    for k in range(4):
                        pe.wait_ge(w_lo, n0 + k + 1)
                        for g in range(NG):
                            feature_unit(k % 2, f0 + k, g)
                    pe.wait_ge(f_lo, 6 * (2 * i + odd + 1))
                    for hf in range(2):
                        pe.wait_ge(w_lo, n0 + 4 + hf + 1)
                        row_units(hf, 8 + 4 * i + 2 * odd + hf, hf, odd)
            pe.wait_ge(f_lo, 6 * NCH)
            for hf in range(2):
                pe.wait_ge(w_lo, FFN_SLAB + 64 + hf + 1)
                row_units(hf, 8 + 2 * (NCH - 1) + hf, hf, 0)


_INS = ["x_prompt", "x_sample", "state_conv", "cache_k", "cache_v", "norm_mix_w", "w_in", "conv_w", "q_norm_w",
        "k_norm_w", "sinks", "w_out", "norm_ffn_w", "w_gate", "w_up", "w_down"]
_OUTS = [("y_prompt", (1, SEQ, D)), ("y_sample", (DEC_B, DEC_T, D)), ("new_conv_prompt", (1, 1, 2, D)),
         ("new_k_prompt", (1, 1, P, NKV, HD)), ("new_v_prompt", (1, 1, P, NKV, HD)),
         ("new_conv_sample", (1, DEC_B, 2, D)), ("new_k_sample", (1, DEC_B, DEC_T, NKV, HD)),
         ("new_v_sample", (1, DEC_B, DEC_T, NKV, HD))]


def kernel(**inputs):
    from concourse import bacc
    from concourse.bass_utils import run_bass_kernel_spmd

    nc = bacc.Bacc("TRN2", target_bir_lowering=False, num_devices=1)
    arrays, io = {}, {}
    for name in _INS:
        a = np.ascontiguousarray(inputs[name])
        arrays[f"in_{name}"] = a
        io[name] = nc.dram_tensor(f"in_{name}", a.shape, mybir.dt.from_np(a.dtype), kind="ExternalInput").ap()
    for name, shape in _OUTS:
        io[name] = nc.dram_tensor(f"out_{name}", shape, F32, kind="ExternalOutput").ap()
    build(nc, io)
    r = run_bass_kernel_spmd(nc, [arrays], core_ids=[0])
    return tuple(r.results[0][f"out_{name}"] for name, _ in _OUTS)
```

```python
from contextlib import ExitStack

import numpy as np

import concourse.bass as bass
from concourse import mybir

F32, F32R, BF16 = mybir.dt.float32, mybir.dt.float32r, mybir.dt.bfloat16
ALU = mybir.AluOpType
ACT = mybir.ActivationFunctionType
AX_X = mybir.AxisListType.X

P = 128
D = 1024
SEQ = 1024
DEC_B, DEC_T = 8, 16
TOK = SEQ + DEC_B * DEC_T
NT = TOK // P
NG = 3
G = TOK // NG
KT = D // P
HD = 64
NH, NKV = D // HD, 4
D_FF = 2816
FC = 256
NCH = D_FF // FC
EPS = 1e-6
NEG = -1e30
H_OFF, B_OFF, C_OFF, Q_OFF = 0, D, 2 * D, 3 * D
K_OFF = 4 * D
V_OFF = K_OFF + NKV * HD
GC_OFF = V_OFF + NKV * HD
GA_OFF = GC_OFF + D
UP0 = 2 + SEQ
UW = UP0 + DEC_B * (2 + DEC_T)
SLAB = KT * P
Q_SLAB = 4
PAIR_SLAB = 12
OUT_SLAB = 52
FFN_SLAB = 60
STEPS = 8
SLOTS = 3 * STEPS
PASSES = ((0, 0), (0, 1), (1, 0))
DU = 5


LEAD = 3
LAST_ROWS = [(hf, t - LEAD * hf) for t in range(NT + LEAD) for hf in range(2) if 0 <= t - LEAD * hf < NT]
LAST_POS = {ht: n for n, ht in enumerate(LAST_ROWS)}
LAST_BASE = 6 * NT


def norm_bank(ph, t, h):
    if ph == 0:
        return 5 + (2 * t + h) % 3
    return (2 * t + h) % 3 if t < 7 else (5, 6, 7, 3)[2 * (t - 7) + h]


class Slab:

    def __init__(self, first, per=0, i=0):
        self.n = first + per * i
        self.slot = first % 2
        self.turn = first // 2 + (per // 2) * i


def build(nc, io):
    ctx = ExitStack()
    with ctx:
        def sb(name, shape, dt=F32):
            return ctx.enter_context(nc.sbuf_tensor(name, shape, dt))

        def sem(name):
            return ctx.enter_context(nc.semaphore(name))

        def overlay(name, nbytes, *groups):
            out = []
            for group in groups:
                with ExitStack() as inner:
                    out.append([inner.enter_context(nc.sbuf_tensor(n, s, d)) for n, s, d in group])
            ctx.enter_context(nc.sbuf_tensor(name, [P, nbytes // 4], F32))
            return out

        xs = [sb("x_hi", [P, KT, TOK], F32R), sb("x_lo", [P, KT, TOK], F32R)]
        ([O], [xn_f, scratch_f, wbc_f, Gt, Ht]) = overlay(
            "o_space", KT * TOK * 4,
            [("O", [P, KT, TOK], F32)],
            [("xn_f", [P, 2, D], F32), ("scratch_f", [P, D], F32), ("wbc_f", [P, D], F32),
             ("silu_gate", [P, 2, TOK], F32), ("ffn_h", [P, 2, G], F32)])
        ([X], [V, kT, qst, kst, vst, ck, cv, ks, ksmp, vsmp, qs, mask, window, halves, ones_row]) = overlay(
            "x_space", NT * D * 4,
            [("X", [P, NT, D], F32)],
            [("V", [P, NT + 1, NKV * HD], F32), ("kT", [P, 2, P + TOK], F32),
             ("q_stage", [P, 2, 4, P], F32), ("k_stage", [P, 2, 2 * P], F32), ("v_stage", [P, 2, 2, P], F32),
             ("cache_k_rows", [P, 2, P], F32), ("cache_v_rows", [P, 2, P], F32), ("cache_kT", [P, 2, P], F32),
             ("sample_kT", [P, P], F32), ("sample_v", [P, P], F32), ("q_sample", [P, 2, 4, DEC_T], F32),
             ("mask", [2, 3, 2 * P], BF16), ("window", [1, 2 * P - DEC_T], BF16),
             ("halves", [2, P], BF16), ("ones_row", [1, P], BF16)])
        act_bytes = 2 * 2 * TOK * 4
        ([xn_p, scratch_p, wbc_p, blockones], [Pb, PT, sqst, sqs], [act0]) = overlay(
            "act0_space", act_bytes,
            [("xn_p", [P, 2, D], F32), ("scratch_p", [P, D], F32), ("wbc_p", [P, D], F32), ("blockones", [P, P], F32)],
            [("probs", [P, 2, 4, 2 * P], F32), ("probsT", [P, 2, 4, P], F32), ("q_sq", [P, 4, P], F32),
             ("q_sample_sq", [P, 4, DEC_T], F32)],
            [("act0", [P, 2, 2, TOK], F32R)])
        ([A, U, S], [act1]) = overlay(
            "act1_space", act_bytes,
            [("branch", [P, 2, TOK], F32), ("u", [P, UW], F32), ("gate", [P, 2, G], F32)],
            [("act1", [P, 2, 2, TOK], F32R)])
        acts = [act0, act1]
        raw = [sb(f"w_raw{i}", [P, SLAB]) for i in range(2)]
        ws = [[sb(f"w_hi{i}", [P, SLAB], F32R), sb(f"w_lo{i}", [P, SLAB], F32R)] for i in range(2)]
        ident = sb("ident", [P, P])
        ones2 = sb("ones2", [P, 2])
        tails = sb("tails", [P, KT, 2 + 2 * DEC_B])
        stT = sb("stT", [P, DEC_B, 2, KT])
        cwT = sb("cwT", [P, 3, KT])
        qnw = sb("qnw", [P, 1])
        knw = sb("knw", [P, 1])
        eps = sb("eps", [P, 1])
        sinkb = sb("sinkb", [P, NH])
        sinkS = sb("sinkS", [P, 2])
        neghalf = sb("neghalf", [P, 9])
        ss = sb("ss", [P, NT])
        sd = sb("sd", [P, NT])
        rms = sb("rms", [P, NT])
        ms = sb("ms", [P, 2, 9])
        rs = sb("rs", [P, 2, 9])
        soft = sb("soft", [P, 9, 4])
        kr = A[:, 0, :].rearrange("p (r g) -> p r g", r=NG)
        kout = A[:, 1, 0:4 * P].rearrange("p (t c) -> p t c", t=2)
        rows_st, rows_cw = A[:, 1, 4 * P:5 * P], A[0:24, 1, 5 * P:6 * P]
        tout = U[0:2 + 2 * DEC_B, 0:D]

        banks = ctx.enter_context(nc.psum_tensor("banks", [P, 8, 512], F32))
        scores = banks[:, 3:5, :].rearrange("p b (h k) -> p (b h) k", k=2 * P)

        const_in = sem("const_in")
        x_in = [sem(f"x_in{t}") for t in range(NT)]
        raw_in = [sem("raw_in0"), sem("raw_in1")]
        cache_in = [sem("cache_in0"), sem("cache_in1")]
        wbc_in = sem("wbc_in")
        consts_made = sem("consts_made")
        w_hi, w_lo = sem("w_hi_ready"), sem("w_lo_ready")
        sq_done, sd_done, rms_done, xn_ready = sem("sq_done"), sem("sd_done"), sem("rms_done"), sem("xn_ready")
        nT_done, norm_hi, norm_lo = sem("nT_done"), sem("norm_hi"), sem("norm_lo")
        gemm_ready = sem("gemm_ready")
        bank_free = [sem(f"bank_free{g}") for g in range(NG)]
        smallT, small_done = sem("smallT"), sem("small_done")
        vt_ready, v_done = sem("vt_ready"), sem("v_done")
        k_ms, k_sd, k_rs = sem("k_ms"), sem("k_sd"), sem("k_rs")
        kt_ready, kout_done = sem("kt_ready"), sem("kout_done")
        pads_done, masks_done = sem("pads_done"), sem("masks_done")
        staged = sem("staged")
        s0_done, s0_used, rs_ready = sem("s0_done"), sem("s0_used"), sem("rs_ready")
        s1_done, s2_done, s3_done = sem("scores_done"), sem("probsT_done"), sem("pv_done")
        soft_done, exp_done, p_ready = sem("soft_done"), sem("exp_done"), sem("p_ready")
        pt_ready, o_done = sem("pt_ready"), sem("o_done")
        conv_step, sg_used, merged = sem("conv_step"), sem("sg_used"), sem("merged")
        tail_step, tailsT, tout_done = sem("tail_step"), sem("tailsT"), sem("tout_done")
        m_hi, m_lo = sem("m_hi"), sem("m_lo")
        d_ready, d_free = sem("d_ready"), sem("d_free")
        f_hi, f_lo = sem("f_hi"), sem("f_lo")
        small_out, y_out = sem("small_out"), sem("y_out")
        kstore_out = sem("kstore_out")

        w_in = io["w_in"][0].rearrange("(k p) c -> p k c", p=P)
        w_q = io["w_in"][0][:, Q_OFF:Q_OFF + D].rearrange("(k p) (a s j d) -> p k a s j d", p=P, a=2, s=2, j=4)
        w_gate = io["w_gate"][0].rearrange("(k p) c -> p k c", p=P)
        w_up = io["w_up"][0].rearrange("(k p) c -> p k c", p=P)
        w_out = io["w_out"][0].rearrange("(k p) n -> p k n", p=P)
        w_down = io["w_down"][0].rearrange("(k p) n -> p k n", p=P)
        xp = io["x_prompt"][0].rearrange("(t p) d -> t p d", p=P)
        xsm = io["x_sample"].rearrange("b t d -> (b t) d")
        yp = io["y_prompt"][0].rearrange("(t p) d -> t p d", p=P)
        ysm = io["y_sample"].rearrange("b t d -> (b t) d")
        cache_k = io["cache_k"][0].rearrange("b n h d -> b n (h d)")
        cache_v = io["cache_v"][0].rearrange("b n h d -> b n (h d)")

        def slab_is_done(eng, kind, idx):
            if kind == "u":
                eng.wait_ge(gemm_ready, idx)
            elif kind == "du":
                eng.wait_ge(d_ready, idx)
            elif kind == "f":
                eng.wait_ge(gemm_ready, 3 * (idx + 1))
            else:
                eng.wait_ge(d_ready, NT * (idx + 1))

        block = ctx.enter_context(nc.Block())

        @block.sync
        def _(sp):
            def load(slab, halves_of):
                if not (isinstance(slab.n, int) and slab.n < 2):
                    sp.wait_ge(w_lo, slab.n - 1)
                for dst, src in halves_of:
                    sp.dma_start(dst, src).then_inc(raw_in[slab.slot], 16)

            def cols(slab, w, c0):
                dst = raw[slab.slot][:, :].rearrange("p (k c) -> p k c", k=KT)
                load(slab, [(dst[:, h:h + 4, :], w[:, h:h + 4, bass.ds(c0, P)]) for h in (0, 4)])

            sp.dma_start(X[:, 0, :], xp[0]).then_inc(x_in[0], 16)
            sp.dma_start(wbc_p[:, :], io["norm_mix_w"][0].partition_broadcast(P)).then_inc(wbc_in, 16)
            sp.dma_start(X[:, 1, :], xp[1]).then_inc(x_in[1], 16)
            cols(Slab(0), w_in, V_OFF)
            for t in range(2, 5):
                sp.dma_start(X[:, t, :], xp[t]).then_inc(x_in[t], 16)
            cols(Slab(1), w_in, V_OFF + P)
            for t in range(5, NT):
                sp.dma_start(X[:, t, :], xp[t] if t < NT - 1 else xsm).then_inc(x_in[t], 16)
            cols(Slab(2), w_in, K_OFF)
            cols(Slab(3), w_in, K_OFF + P)
            with sp.Fori(0, 2) as i:
                for j in range(4):
                    slab = Slab(Q_SLAB + j, 4, i)
                    dst = raw[slab.slot][:, :].rearrange("p (k s c) -> p k s c", k=KT, s=2)
                    load(slab, [(dst[:, :, h, :], w_q[:, :, bass.ds(i, 1), h, j, :].rearrange("p k a d -> p k (a d)"))
                                for h in range(2)])

            def pair_loads(i):
                for jj in range(2):
                    for c, off in enumerate((H_OFF, C_OFF, B_OFF, GC_OFF)):
                        cols(Slab(PAIR_SLAB + 4 * jj + c, 10, i), w_in, off + (2 * i + jj) * P)
                for jj in range(2):
                    cols(Slab(PAIR_SLAB + 8 + jj, 10, i), w_in, GA_OFF + (2 * i + jj) * P)

            with sp.Fori(0, 2) as i:
                pair_loads(i)
            with sp.Fori(2, 4) as i:
                pair_loads(i)

            def rows(slab, w, k0, hf):
                load(slab, [(raw[slab.slot][:, k * 512:(k + 1) * 512],
                             w[:, bass.ds(k0 + k, 1), hf * 512:(hf + 1) * 512].rearrange("p a c -> p (a c)"))
                            for k in range(2)])

            sp.wait_ge(o_done, 2 * SLOTS)
            sp.wait_ge(small_out, 32)
            for t in range(NT):
                sp.dma_start(X[:, t, :], xp[t] if t < NT - 1 else xsm).then_inc(x_in[t], 16)
            for c in range(4):
                for hf in range(2):
                    rows(Slab(OUT_SLAB + 2 * c + hf), w_out, 2 * c, hf)
            sp.wait_ge(m_lo, 4)
            sp.dma_start(wbc_f[:, :], io["norm_ffn_w"][0].partition_broadcast(P)).then_inc(wbc_in, 16)

            def gate_up(first, per, i, c):
                for b in range(2):
                    cols(Slab(first + 2 * b, per, i), w_gate, c * FC + b * P)
                    cols(Slab(first + 2 * b + 1, per, i), w_up, c * FC + b * P)

            def down(first, per, i, c):
                for hf in range(2):
                    rows(Slab(first + hf, per, i), w_down, 2 * c, hf)

            gate_up(FFN_SLAB, 0, 0, 0)
            with sp.Fori(0, (NCH - 1) // 2) as i:
                gate_up(FFN_SLAB + 4, 12, i, 2 * i + 1)
                down(FFN_SLAB + 8, 12, i, 2 * i)
                gate_up(FFN_SLAB + 10, 12, i, 2 * i + 2)
                down(FFN_SLAB + 14, 12, i, 2 * i + 1)
            down(FFN_SLAB + 64, 0, 0, NCH - 1)
            for hf in range(2):
                for t in range(NT):
                    sp.wait_ge(d_free, NT * (8 + 2 * (NCH - 1) + hf) + t + 1)
                    dst = yp[t] if t < NT - 1 else ysm
                    sp.dma_start(dst[:, hf * 512:(hf + 1) * 512], X[:, t, hf * 512:(hf + 1) * 512]).then_inc(y_out, 16)
            sp.wait_ge(y_out, 16 * 2 * NT)

        @block.gpsimd
        def _(gp):
            gp.dma_start(rows_st, io["state_conv"][0].rearrange("b r (j c) -> (b r j) c", c=P)).then_inc(const_in, 16)
            gp.dma_start(rows_cw, io["conv_w"][0].rearrange("w (j c) -> (w j) c", c=P)).then_inc(const_in, 16)
            for s in range(2):
                gp.dma_start(qnw[HD * s:HD * (s + 1), :], io["q_norm_w"].rearrange("a d -> d a")).then_inc(const_in, 16)
                gp.dma_start(knw[HD * s:HD * (s + 1), :], io["k_norm_w"].rearrange("a d -> d a")).then_inc(const_in, 16)
            gp.dma_start(sinkb[:, :], io["sinks"][0].partition_broadcast(P)).then_inc(const_in, 16)
            sink_rows = io["sinks"][0].rearrange("(a r) -> r a", a=2)
            for r in range(8):
                gp.dma_start(sinkS[DEC_T * r:DEC_T * (r + 1), :], sink_rows[r].partition_broadcast(DEC_T),
                             allow_slow_non_contiguous=True).then_inc(const_in, 16)
            gp.memset(ident[:, :], 0.0).then_inc(consts_made, 1)
            gp.wait_ge(consts_made, 1)
            gp.affine_select(out=ident[:, :], in_=ident[:, :], compare_op=ALU.not_equal, fill=1.0, base=0,
                             pattern=[[-1, P]], channel_multiplier=1).then_inc(consts_made, 1)
            gp.memset(eps[:, :], EPS).then_inc(consts_made, 1)
            gp.memset(blockones[:, :], 0.0).then_inc(consts_made, 1)
            gp.memset(ones2[:, :], 0.0).then_inc(consts_made, 1)
            gp.memset(neghalf[:, :], -0.5).then_inc(consts_made, 1)
            gp.wait_ge(consts_made, 6)
            for s in range(2):
                half = slice(HD * s, HD * (s + 1))
                gp.memset(blockones[half, half], 1.0).then_inc(consts_made, 1)
                gp.memset(ones2[half, s:s + 1], 1.0).then_inc(consts_made, 1)

            def split_lo(slab):
                gp.wait_ge(w_hi, slab.n + 1)
                gp.tensor_tensor(ws[slab.slot][1][:, :], raw[slab.slot][:, :], ws[slab.slot][0][:, :].bitcast(F32),
                                 ALU.subtract).then_inc(w_lo, 1)

            for n in range(3):
                split_lo(Slab(n))
            gp.wait_ge(norm_lo, 2 * NT)
            gp.memset(V[:, 0, :], 0.0).then_inc(pads_done, 1)
            for a in range(2):
                gp.memset(kT[:, a, 0:P], 0.0).then_inc(pads_done, 1)
            gp.memset(mask[:, :, :], 0.0).then_inc(masks_done, 1)
            gp.memset(halves[:, :], 1.0).then_inc(masks_done, 1)
            gp.memset(ones_row[:, :], 1.0).then_inc(masks_done, 1)
            gp.memset(window[:, :], NEG).then_inc(masks_done, 1)
            gp.wait_ge(masks_done, 4)
            for v in (1, 2):
                gp.affine_select(out=mask[:, v, :], in_=mask[:, v, :], compare_op=ALU.is_ge, fill=NEG, base=0,
                                 pattern=[[1, 2 * P]], channel_multiplier=-HD).then_inc(masks_done, 1)
            gp.affine_select(out=mask[:, 0, :], in_=mask[:, 0, :], compare_op=ALU.is_ge, fill=NEG, base=-P,
                             pattern=[[1, 2 * P]], channel_multiplier=0).then_inc(masks_done, 1)
            gp.affine_select(out=halves[:, :], in_=halves[:, :], compare_op=ALU.is_ge, fill=0.0, base=0,
                             pattern=[[1, P]], channel_multiplier=-HD).then_inc(masks_done, 1)
            gp.memset(window[:, P - DEC_T:P], 0.0).then_inc(masks_done, 1)
            gp.wait_ge(masks_done, 9)
            for v in range(3):
                gp.affine_select(out=mask[:, v, :], in_=mask[:, v, :], compare_op=ALU.is_ge, fill=NEG, base=3 * HD - 1,
                                 pattern=[[-1, 2 * P]], channel_multiplier=HD).then_inc(masks_done, 1)
            gp.affine_select(out=halves[:, :], in_=halves[:, :], compare_op=ALU.is_ge, fill=0.0, base=HD - 1,
                             pattern=[[-1, P]], channel_multiplier=HD).then_inc(masks_done, 1)
            split_lo(Slab(3))
            split_lo(Slab(4))
            gp.wait_ge(v_done, 6)
            gp.dma_start(io["new_v_prompt"][0, 0].rearrange("n h d -> n (h d)"), V[:, NT - 1, :]).then_inc(small_out, 16)
            gp.dma_start(io["new_v_sample"][0].rearrange("b n h d -> (b n) (h d)"), V[:, NT, :]).then_inc(small_out, 16)
            with gp.Fori(0, 2) as i:
                for j in range(4):
                    split_lo(Slab(Q_SLAB + j + 1, 4, i))

            def stage(i, t):
                par, q = t % 2, STEPS * i + t
                if t >= 1:
                    gp.wait_ge(s0_done, q)
                if t >= 2:
                    gp.wait_ge(s3_done, 3 * (q - 1))
                for cache, dst in ((cache_k, ck), (cache_v, cv)):
                    gp.dma_start(dst[:, par, :], cache[t][:, bass.ds(i * P, P)]).then_inc(cache_in[par], 16)
                blocks = bass.ds(4 * i, 4)
                q_t = O[:, blocks, t * P:(t + 1) * P]
                q_s = O[:, blocks, SEQ + t * DEC_T:SEQ + (t + 1) * DEC_T]
                gp.tensor_copy(qst[:, par, :, :], q_t)
                gp.tensor_tensor(sqst[:, :, :], q_t, q_t, ALU.mult)
                gp.tensor_copy(qs[:, par, :, :], q_s)
                gp.tensor_tensor(sqs[:, :, :], q_s, q_s, ALU.mult)
                gp.tensor_tensor(kst[:, par, :], kT[:, bass.ds(i, 1), t * P:(t + 2) * P].rearrange("p a k -> p (a k)"),
                                 qnw[:, :].broadcast_to([P, 2 * P]), ALU.mult)
                if t == 0:
                    gp.tensor_tensor(ksmp[:, :], kT[:, bass.ds(i, 1), SEQ + P:SEQ + 2 * P].rearrange("p a k -> p (a k)"),
                                     qnw[:, :].broadcast_to([P, P]), ALU.mult)
                    gp.tensor_copy(vsmp[:, :], V[:, NT, bass.ds(i * P, P)])
                gp.tensor_copy(vst[:, par, :, :], V[:, t:t + 2, bass.ds(i * P, P)]).then_inc(staged, 1)

            def q_rms(i, t):
                par, q = t % 2, STEPS * i + t
                gp.wait_ge(s0_used, q + 1)
                gp.tensor_tensor(rs[:, par, :], ms[:, par, :], neghalf[:, :], ALU.pow).then_inc(rs_ready, 1)

            for g in range(NG):
                gp.wait_ge(bank_free[g], Q_SLAB + 4)
            gp.wait_ge(pads_done, 3)
            gp.wait_ge(const_in, 16 * 15)
            gp.wait_ge(consts_made, 10)
            with gp.Fori(0, 2) as i:
                stage(i, 0)
                q_rms(i, 0)
                for t in range(STEPS):
                    split_lo(Slab(PAIR_SLAB + t + 1, 10, i))
                    if t + 1 < STEPS:
                        stage(i, t + 1)
                        q_rms(i, t + 1)
                for jj in range(2):
                    split_lo(Slab(PAIR_SLAB + 9 + jj, 10, i))
            with gp.Fori(2, 4) as i:
                for c in range(10):
                    split_lo(Slab(PAIR_SLAB + c + 1, 10, i))
            gp.wait_ge(tout_done, 2)
            gp.dma_start(io["new_conv_prompt"][0, 0], tout[0:2, :]).then_inc(small_out, 16)
            gp.dma_start(io["new_conv_sample"][0].rearrange("b r c -> (b r) c"), tout[2:2 + 2 * DEC_B, :])\
                .then_inc(small_out, 16)
            for n in range(OUT_SLAB + 1, FFN_SLAB + 4 + 1):
                split_lo(Slab(n))
            with gp.Fori(0, (NCH - 1) // 2) as i:
                for c in range(12):
                    split_lo(Slab(FFN_SLAB + 5 + c, 12, i))
            split_lo(Slab(FFN_SLAB + 65))
            gp.wait_ge(small_out, 64)

        @block.scalar
        def _(act):
            def split_hi(slab, *free):
                act.wait_ge(raw_in[slab.slot], 32 * (slab.turn + 1))
                if free:
                    slab_is_done(act, *free)
                act.activation(ws[slab.slot][0][:, :], raw[slab.slot][:, :], ACT.Copy).then_inc(w_hi, 1)

            def norm_stats(ph, t):
                if ph == 0:
                    act.wait_ge(x_in[t], 16)
                else:
                    act.wait_ge(d_free, LAST_BASE + LAST_POS[1, t] + 1)
                q = (NT + 6) * ph + t
                if q:
                    act.wait_ge(sq_done, q)
                scratch = (scratch_p, scratch_f)[ph]
                act.activation(scratch[:, :], X[:, t, :], ACT.Square, accum_out=ss[:, t:t + 1]).then_inc(sq_done, 1)
                act.wait_ge(sq_done, q + 1)
                act.activation(sd[:, t:t + 1], ss[:, t:t + 1], ACT.Sqrt, bias=eps[:, :], scale=1.0 / D).then_inc(sd_done, 1)

            def norm_hi_part(ph, t):
                for h in range(2):
                    idx = 2 * (NT * ph + t) + h
                    act.wait_ge(nT_done, idx + 1)
                    src = banks[:, norm_bank(ph, t, h), :].rearrange("p (k c) -> p k c", k=4)
                    act.activation(xs[0][:, 4 * h:4 * h + 4, t * P:(t + 1) * P], src, ACT.Copy).then_inc(norm_hi, 1)

            act.wait_ge(consts_made, 10)
            norm_stats(0, 0)
            split_hi(Slab(0))
            norm_stats(0, 1)

            def v_evac(x):
                act.wait_ge(gemm_ready, x + 1)
                if x >= 2:
                    act.wait_ge(vt_ready, x - 1)
                act.activation(S[:, x % 2, :], banks[:, x % 3, 0:G], ACT.Copy).then_inc(bank_free[x % 3], 1)

            for t in range(NT):
                norm_hi_part(0, t)
                if t + 2 < NT:
                    norm_stats(0, t + 2)
                if t == 0:
                    split_hi(Slab(1))
                if t in (3, 5, 6, 8):
                    v_evac((3, 5, 6, 8).index(t))
            v_evac(4)
            split_hi(Slab(2), "u", 5)
            v_evac(5)
            split_hi(Slab(3), "u", 6)

            def k_root(w):
                act.wait_ge(k_ms, w + 1)
                if w >= 3:
                    act.wait_ge(bank_free[w % 3], 3)
                act.activation(kr[:, w % 3, :], banks[:, 3 + w % 2, 0:G], ACT.Sqrt, bias=eps[:, :],
                               scale=1.0 / HD).then_inc(k_sd, 1)

            for w in range(6):
                g = w % 3
                act.wait_ge(gemm_ready, 6 + w + 1)
                if w >= 2:
                    act.wait_ge(k_ms, w - 1)
                else:
                    act.wait_ge(vt_ready, 6)
                act.activation(S[:, w % 2, :], banks[:, g, 0:G], ACT.Square).then_inc(sq_done, 1)
                k_root(w)
                if w == 2:
                    split_hi(Slab(4), "f", 2)

            with act.Fori(0, 2) as i:
                for j in range(4):
                    split_hi(Slab(Q_SLAB + j + 1, 4, i), "f", Q_SLAB + 4 * i + j - 1)
                    for g in range(NG):
                        act.wait_ge(gemm_ready, 3 * (Q_SLAB + 4 * i + j) + g + 1)
                        act.activation(O[:, bass.ds(4 * i + j, 1), g * G:(g + 1) * G].rearrange("p a c -> p (a c)"),
                                       banks[:, g, 0:G], ACT.Copy).then_inc(bank_free[g], 1)

            act.wait_ge(kout_done, 1)
            act.dma_start(io["new_k_prompt"][0, 0].rearrange("n h d -> n (h d)"), kout[:, 0, :]).then_inc(kstore_out, 16)
            act.dma_start(io["new_k_sample"][0].rearrange("b n h d -> (b n) (h d)"), kout[:, 1, :])\
                .then_inc(kstore_out, 16)
            act.wait_ge(kstore_out, 32)

            def out_attention(i, t, u):
                z = SLOTS * i + 3 * t + u
                act.wait_ge(s3_done, z + 1)
                if u < 2:
                    dst = O[:, bass.ds(4 * i + 2 * u, 2), t * P:(t + 1) * P]
                    src = banks[:, 7, 0:2 * P].rearrange("p (b q) -> p b q", b=2)
                else:
                    dst = O[:, bass.ds(4 * i, 4), SEQ + t * DEC_T:SEQ + (t + 1) * DEC_T]
                    src = banks[:, 7, 0:4 * DEC_T].rearrange("p (b q) -> p b q", b=4)
                act.activation(dst, src, ACT.Copy, scale=0.5).then_inc(o_done, 1)

            def exps(i, t, u):
                z, par = SLOTS * i + 3 * t + u, t % 2
                p = Pb[:, (3 * t + u) % 2]
                n = 4 if u < 2 else 1
                act.wait_ge(soft_done, 7 * z + 5)
                for h in range(n):
                    scale = rs[:, par, 2 * h + u:2 * h + u + 1] if u < 2 else rs[:, par, 8:9]
                    act.activation(p[:, h, :], scores[:, h, :], ACT.Exp, bias=soft[:, 3, h:h + 1], scale=scale,
                                   accum_out=soft[:, 5, h:h + 1])
                act.activation(soft[:, 6, 0:n], soft[:, 4, 0:n], ACT.Exp).then_inc(exp_done, 1)
                act.wait_ge(soft_done, 7 * z + 7)
                for h in range(n):
                    ins = act.activation(p[:, h, :], p[:, h, :], ACT.Copy, scale=soft[:, 8, h:h + 1])
                ins.then_inc(p_ready, 1)

            def unit(i, c, g):
                f = PAIR_SLAB + 10 * i + c
                bank = banks[:, g, 0:G]
                jj, kind = (c // 4, c % 4) if c < 8 else (c - 8, 4)
                if kind == 0:
                    act.wait_ge(gemm_ready, 3 * f + g + 1)
                    act.wait_ge(merged, 6 * i + 1)
                    act.activation(A[:, jj, g * G:(g + 1) * G], bank, ACT.Copy).then_inc(bank_free[g], 1)
                elif kind >= 3:
                    e = 12 * i + (3 * jj if kind == 3 else 6 + 3 * jj) + g
                    act.wait_ge(gemm_ready, 3 * f + g + 1)
                    slot = (3 * jj + g) % 2
                    if c > 3 or g > 1:
                        act.wait_ge(sg_used, e - 1)
                    act.activation(S[:, slot, :], bank, ACT.Tanh, scale=0.5).then_inc(bank_free[g], 1)

            with act.Fori(0, 2) as i:
                for t in range(STEPS):
                    split_hi(Slab(PAIR_SLAB + t + 1, 10, i), "f", PAIR_SLAB + 10 * i + t - 1)
                    for u in range(3):
                        exps(i, t, u)
                        unit(i, t, u)
                        if 3 * t + u:
                            out_attention(i, *((t, u - 1) if u else (t - 1, 2)))
                split_hi(Slab(PAIR_SLAB + 9, 10, i), "f", PAIR_SLAB + 10 * i + 7)
                out_attention(i, STEPS - 1, 2)
                for g in range(NG):
                    unit(i, 8, g)
                split_hi(Slab(PAIR_SLAB + 10, 10, i), "f", PAIR_SLAB + 10 * i + 8)
                for g in range(NG):
                    unit(i, 9, g)

            def merged_hi(c):
                act.wait_ge(merged, 1 + (6 * (c + 1) if c != 1 else 24))
                if c == 1:
                    act.wait_ge(small_out, 64)
                if c >= 2:
                    slab_is_done(act, "d", 2 * (c - 2) + 1)
                act.activation(acts[c % 2][:, :, 0, :], O[:, 2 * c:2 * c + 2, :], ACT.Copy).then_inc(m_hi, 1)

            merged_hi(0)
            with act.Fori(2, 4) as i:
                for c in range(10):
                    split_hi(Slab(PAIR_SLAB + c + 1, 10, i), "f", PAIR_SLAB + 10 * i + c - 1)
                    for g in range(NG):
                        unit(i, c, g)

            for c in range(4):
                for hf in range(2):
                    n = 2 * c + hf
                    if n < 7:
                        split_hi(Slab(OUT_SLAB + n + 1), *(("d", n - 1) if n else ("f", OUT_SLAB - 1)))
                    if hf == 0 and c < 3:
                        merged_hi(c + 1)

            def gate(first, per, i, b, g):
                f = first + per * i
                act.wait_ge(gemm_ready, 3 * f + g + 1)
                act.activation(Gt[:, b, g * G:(g + 1) * G], banks[:, g, 0:G], ACT.Silu).then_inc(bank_free[g], 1)

            def up(first, per, i, slot, b, g):
                f = first + per * i
                act.wait_ge(bank_free[g], f + 1)
                act.activation(acts[slot][:, b, 0, g * G:(g + 1) * G], Ht[:, (3 * b + g) % 2, :], ACT.Copy)\
                    .then_inc(f_hi, 1)

            F0 = OUT_SLAB
            act.wait_ge(m_lo, 4)
            for t in range(NT):
                norm_stats(1, t)
                if t >= 2:
                    norm_hi_part(1, t - 2)
                if t == NT - 2:
                    split_hi(Slab(FFN_SLAB), "du", LAST_BASE + LAST_POS[0, NT - 1] + 1)
            split_hi(Slab(FFN_SLAB + 1), "d", 7)

            def gate_up_turn(g):
                x = 2 * g
                act.wait_ge(gemm_ready, 3 * F0 + x + 1)
                act.activation(Gt[:, 0, g * G:(g + 1) * G], banks[:, x % 3, 0:G], ACT.Silu)\
                    .then_inc(bank_free[x % 3], 1)
                act.wait_ge(bank_free[(x + 1) % 3], F0 + (x + 1) // 3 + 1)
                act.activation(acts[0][:, 0, 0, g * G:(g + 1) * G], Ht[:, g % 2, :], ACT.Copy).then_inc(f_hi, 1)

            for g in range(NG):
                gate_up_turn(g)
                if g < 2:
                    norm_hi_part(1, 7 + g)
            split_hi(Slab(FFN_SLAB + 2), "u", 3 * F0 + 5)
            split_hi(Slab(FFN_SLAB + 3), "f", F0 + 1)
            for g in range(NG):
                gate(F0 + 2, 0, 0, 1, g)
            split_hi(Slab(FFN_SLAB + 4), "f", F0 + 2)
            for g in range(NG):
                up(F0 + 3, 0, 0, 0, 1, g)

            with act.Fori(0, (NCH - 1) // 2) as i:
                for odd in range(2):
                    n0 = FFN_SLAB + 4 + 6 * odd
                    f0 = F0 + 4 + 4 * odd
                    s0 = 8 + 2 * odd
                    slot = 1 - odd
                    for b in range(2):
                        for k in range(2):
                            idx = 2 * b + k
                            if idx == 0:
                                if odd:
                                    free = ("d", s0 - 2 + 4 * i + 1)
                                else:
                                    free = None
                            else:
                                free = ("f", f0 + idx - 1 + 8 * i)
                            if free is None:
                                act.wait_ge(gemm_ready, 3 * (F0 + 4 + 8 * i))
                                act.wait_ge(d_ready, NT * (8 + 4 * i))
                                split_hi(Slab(n0 + 1, 12, i))
                            else:
                                split_hi(Slab(n0 + idx + 1, 12, i), *free)
                            for g in range(NG):
                                if k == 0:
                                    gate(f0 + idx, 8, i, b, g)
                                else:
                                    up(f0 + idx, 8, i, slot, b, g)
                    split_hi(Slab(n0 + 5, 12, i), "f", f0 + 3 + 8 * i)
                    split_hi(Slab(n0 + 6, 12, i), "d", s0 + 4 * i)
            split_hi(Slab(FFN_SLAB + 65), "d", 8 + 2 * (NCH - 1) - 1)

        @block.vector
        def _(dve):
            def norm_scale(ph, t):
                xn, wbc = ((xn_p, wbc_p), (xn_f, wbc_f))[ph]
                q = NT * ph + t
                dve.wait_ge(sd_done, q + 1)
                dve.reciprocal(rms[:, t:t + 1], sd[:, t:t + 1]).then_inc(rms_done, 1)
                if t >= 2:
                    dve.wait_ge(nT_done, 2 * (q - 1))
                dve.wait_ge(rms_done, q + 1)
                dve.scalar_tensor_tensor(out=xn[:, t % 2, :], in0=X[:, t, :], scalar=rms[:, t:t + 1], in1=wbc[:, :],
                                         op0=ALU.mult, op1=ALU.mult).then_inc(xn_ready, 1)

            def norm_lo_part(ph, t):
                for h in range(2):
                    idx = 2 * (NT * ph + t) + h
                    dve.wait_ge(norm_hi, idx + 1)
                    src = banks[:, norm_bank(ph, t, h), :].rearrange("p (k c) -> p k c", k=4)
                    where = (slice(None), slice(4 * h, 4 * h + 4), slice(t * P, (t + 1) * P))
                    dve.tensor_tensor(xs[1][where], src, xs[0][where].bitcast(F32), ALU.subtract).then_inc(norm_lo, 1)

            dve.wait_ge(wbc_in, 16)
            norm_scale(0, 0)
            norm_scale(0, 1)

            def v_rows(x):
                a, g = x % 2, x // 2
                dve.wait_ge(vt_ready, x + 1)
                dve.tensor_copy(V[:, 1 + 3 * g:4 + 3 * g, a * P:(a + 1) * P],
                                banks[:, 3 + x % 2, 0:G].rearrange("p (t c) -> p t c", t=3)).then_inc(v_done, 1)

            for t in range(NT):
                norm_lo_part(0, t)
                if t + 2 < NT:
                    norm_scale(0, t + 2)
                if t in (5, 7, 8):
                    v_rows((5, 7, 8).index(t))
            for x in range(3, 6):
                v_rows(x)
            dve.wait_ge(const_in, 16 * 15)
            for w in range(6):
                a, g = divmod(w, 3)
                dve.wait_ge(k_sd, w + 1)
                dve.reciprocal(kr[:, w % 3, :], kr[:, w % 3, :]).then_inc(k_rs, 1)
                dve.wait_ge(k_rs, w + 1)
                dve.scalar_tensor_tensor(out=kT[:, a, P + g * G:P + (g + 1) * G], in0=banks[:, g, 0:G], scalar=knw[:, :],
                                         in1=kr[:, w % 3, :], op0=ALU.mult, op1=ALU.mult).then_inc(bank_free[g], 1)
            dve.wait_ge(smallT, 2)
            dve.tensor_copy(stT[:, :, :, :].rearrange("p b r j -> p (b r j)"), banks[:, 5, 0:P]).then_inc(small_done, 1)
            dve.tensor_scalar(cwT[:, :, :].rearrange("p w j -> p (w j)"), banks[:, 5, P:P + 24], 0.5, None, ALU.mult)\
                .then_inc(small_done, 1)
            dve.wait_ge(kt_ready, 1)
            dve.tensor_copy(kout[:, :, :].rearrange("p t c -> p (t c)"), banks[:, 3, :]).then_inc(kout_done, 1)

            def after_s0(i, t):
                q, par = STEPS * i + t, t % 2
                dve.wait_ge(s0_done, q + 1)
                dve.tensor_scalar(ms[:, par, :], banks[:, 7, 0:9], HD * EPS, None, ALU.add)
                dve.tensor_scalar(ks[:, par, :], banks[:, 7, P:2 * P], qnw[:, :], None, ALU.mult).then_inc(s0_used, 1)

            def out_transposed(i, t, u):
                z = SLOTS * i + 3 * t + u
                dve.wait_ge(s2_done, z + 1)
                n = 4 * P if u < 2 else P
                dst = PT[:, :, :, :].rearrange("p k h q -> p k (h q)")[:, :, 0:n]
                dve.tensor_copy(dst, banks[:, 5:7, 0:n]).then_inc(pt_ready, 1)

            def softmax_bias(i, t, u):
                z, par = SLOTS * i + 3 * t + u, t % 2
                n = 4 if u < 2 else 1
                r = rs[:, par, u:u + 7:2] if u < 2 else rs[:, par, 8:9]
                sink = sinkb[:, bass.ds(8 * i + 4 * u, 4)] if u < 2 else sinkS[:, bass.ds(i, 1)]
                dve.wait_ge(s1_done, z + 1)
                dve.tensor_reduce(soft[:, 0, 0:n], scores[:, 0:n, :], AX_X, ALU.max).then_inc(soft_done, 1)
                dve.wait_ge(rs_ready, STEPS * i + t + 1)
                dve.wait_ge(soft_done, 7 * z + 1)
                dve.tensor_tensor(soft[:, 1, 0:n], soft[:, 0, 0:n], r, ALU.mult).then_inc(soft_done, 1)
                dve.wait_ge(soft_done, 7 * z + 2)
                dve.tensor_tensor(soft[:, 2, 0:n], soft[:, 1, 0:n], sink, ALU.max).then_inc(soft_done, 1)
                dve.wait_ge(soft_done, 7 * z + 3)
                dve.tensor_scalar(soft[:, 3, 0:n], soft[:, 2, 0:n], -1.0, None, ALU.mult).then_inc(soft_done, 1)
                dve.wait_ge(soft_done, 7 * z + 4)
                dve.tensor_tensor(soft[:, 4, 0:n], soft[:, 3, 0:n], sink, ALU.add).then_inc(soft_done, 1)

            def denominator(i, t, u):
                z = SLOTS * i + 3 * t + u
                n = 4 if u < 2 else 1
                dve.wait_ge(exp_done, z + 1)
                dve.tensor_tensor(soft[:, 7, 0:n], soft[:, 5, 0:n], soft[:, 6, 0:n], ALU.add).then_inc(soft_done, 1)
                dve.wait_ge(soft_done, 7 * z + 6)
                dve.reciprocal(soft[:, 8, 0:n], soft[:, 7, 0:n]).then_inc(soft_done, 1)

            def u_parts(g):
                lo, hi = g * G, min((g + 1) * G, SEQ)
                return lo, hi

            def sample_view(buf, off):
                return buf[:, UP0:UW].rearrange("p (b c) -> p b c", b=DEC_B)[:, :, off:off + DEC_T]

            def sample_cols(a):
                return a[:, SEQ:TOK].rearrange("p (b c) -> p b c", b=DEC_B)

            def conv(i, jj, g):
                lo, hi = u_parts(g)
                base = 18 * i + 3 * (3 * jj + g)
                dve.wait_ge(bank_free[g], PAIR_SLAB + 10 * i + 4 * jj + 2)
                for k in range(3):
                    w = cwT[:, k, bass.ds(2 * i + jj, 1)]
                    if k:
                        dve.wait_ge(conv_step, base + k)
                    parts = [(A[:, jj, lo:hi], U[:, lo + k:hi + k])]
                    if g == 2:
                        parts.append((sample_cols(A[:, jj, :]), sample_view(U, k)))
                    for y, src in parts:
                        if k == 0:
                            ins = dve.tensor_scalar(y, src, w, None, ALU.mult)
                        else:
                            ins = dve.scalar_tensor_tensor(out=y, in0=src, scalar=w, in1=y, op0=ALU.mult, op1=ALU.add)
                    ins.then_inc(conv_step, 1)
                if g == 2:
                    j = bass.ds(2 * i + jj, 1)
                    dve.tensor_copy(tails[:, j, 0:2].rearrange("p a r -> p (a r)"), U[:, UP0 - 2:UP0])
                    dve.tensor_copy(tails[:, j, 2:].rearrange("p a (b r) -> p (a b) r", r=2),
                                    sample_view(U, 2)[:, :, DEC_T - 2:DEC_T]).then_inc(tail_step, 1)

            def unit(i, c, g):
                f = PAIR_SLAB + 10 * i + c
                bank = banks[:, g, 0:G]
                jj, kind = (c // 4, c % 4) if c < 8 else (c - 8, 4)
                a = A[:, jj, g * G:(g + 1) * G]
                if kind == 1:
                    lo, hi = u_parts(g)
                    if g == 0:
                        dve.tensor_copy(U[:, UP0:UW].rearrange("p (b c) -> p b c", b=DEC_B)[:, :, 0:2],
                                        stT[:, :, :, bass.ds(2 * i + jj, 1)].rearrange("p b r a -> p b (r a)"))
                    dve.wait_ge(gemm_ready, 3 * f + g + 1)
                    dve.wait_ge(bank_free[g], f)
                    ins = dve.tensor_tensor(U[:, 2 + lo:2 + hi], bank[:, 0:hi - lo], A[:, jj, lo:hi], ALU.mult)
                    if g == 2:
                        ins = dve.tensor_tensor(sample_view(U, 2),
                                                bank[:, hi - lo:G].rearrange("p (b c) -> p b c", b=DEC_B),
                                                sample_cols(A[:, jj, :]), ALU.mult)
                    ins.then_inc(bank_free[g], 1)
                elif kind == 2:
                    dve.wait_ge(gemm_ready, 3 * f + g + 1)
                    dve.wait_ge(conv_step, 18 * i + 9 * (jj + 1))
                    dve.tensor_tensor(a, bank, a, ALU.mult).then_inc(bank_free[g], 1)
                elif kind == 3:
                    dve.wait_ge(bank_free[g], f + 1)
                    dve.scalar_tensor_tensor(out=a, in0=S[:, (3 * jj + g) % 2, :], scalar=1.0, in1=a, op0=ALU.add,
                                             op1=ALU.mult).then_inc(sg_used, 1)
                elif kind == 4:
                    o = O[:, bass.ds(2 * i + jj, 1), g * G:(g + 1) * G].rearrange("p a c -> p (a c)")
                    e = 12 * i + 6 + 3 * jj + g
                    dve.wait_ge(bank_free[g], f + 1)
                    dve.wait_ge(o_done, SLOTS * min2(i))
                    dve.scalar_tensor_tensor(out=o, in0=S[:, (3 * jj + g) % 2, :], scalar=1.0, in1=o, op0=ALU.add,
                                             op1=ALU.mult).then_inc(sg_used, 1)
                    dve.wait_ge(sg_used, e + 1)
                    dve.tensor_tensor(o, o, a, ALU.add).then_inc(merged, 1)

            attention_on = [True]

            def min2(i):
                return i + 1 if attention_on[0] else 2

            dve.wait_ge(small_done, 2)
            dve.memset(U[:, 0:2], 0.0).then_inc(merged, 1)
            with dve.Fori(0, 2) as i:
                after_s0(i, 0)
                for t in range(STEPS):
                    for u in range(3):
                        softmax_bias(i, t, u)
                        if 3 * t + u:
                            bt, bu = (t, u - 1) if u else (t - 1, 2)
                            if bt % 4 == 1:
                                conv(i, bt // 4, bu)
                            out_transposed(i, bt, bu)
                        if u == 2 and t + 1 < STEPS:
                            after_s0(i, t + 1)
                        denominator(i, t, u)
                        unit(i, t, u)
                out_transposed(i, STEPS - 1, 2)
                for jj in range(2):
                    for g in range(NG):
                        unit(i, 8 + jj, g)
            attention_on[0] = False

            def merged_lo(c):
                dve.wait_ge(m_hi, c + 1)
                dve.tensor_tensor(acts[c % 2][:, :, 1, :], O[:, 2 * c:2 * c + 2, :],
                                  acts[c % 2][:, :, 0, :].bitcast(F32), ALU.subtract).then_inc(m_lo, 1)

            merged_lo(0)
            with dve.Fori(2, 4) as i:
                for c in range(10):
                    for g in range(NG):
                        unit(i, c, g)
                        if c % 4 == 1 and c < 8:
                            conv(i, c // 4, g)

            def add_rows(s, hf, x_turn=None):
                for t in range(NT):
                    x = X[:, t, hf * 512:(hf + 1) * 512]
                    dve.wait_ge(d_ready, NT * s + t + 1)
                    if x_turn is not None:
                        dve.wait_ge(x_in[t], x_turn)
                    else:
                        dve.wait_ge(d_free, NT * (s - 2) + t + 1)
                    dve.tensor_tensor(x, banks[:, 3 + t % DU, :], x, ALU.add).then_inc(d_free, 1)

            dve.wait_ge(tailsT, 2)
            for h in range(2):
                dve.tensor_copy(tout[:, h * 512:(h + 1) * 512], banks[0:2 + 2 * DEC_B, h, :]).then_inc(tout_done, 1)
            for c in range(3):
                add_rows(2 * c, 0, 32 if c == 0 else None)
                merged_lo(c + 1)
                add_rows(2 * c + 1, 1, 32 if c == 0 else None)

            dve.wait_ge(wbc_in, 32)
            for n, (hf, t) in enumerate(LAST_ROWS):
                x = X[:, t, hf * 512:(hf + 1) * 512]
                dve.wait_ge(d_ready, LAST_BASE + n + 1)
                dve.wait_ge(d_free, NT * (4 + hf) + t + 1)
                dve.tensor_tensor(x, banks[:, 3 + n % DU, :], x, ALU.add).then_inc(d_free, 1)
                if hf == 1 and t >= 1:
                    norm_scale(1, t - 1)
                if hf == 1 and t >= 2:
                    norm_lo_part(1, t - 2)
            norm_scale(1, NT - 1)

            def up(first, per, i, c, slot, b, g):
                f = first + per * i
                fu = 6 * c + 3 * b + g
                h = Ht[:, (3 * b + g) % 2, :]
                dve.wait_ge(gemm_ready, 3 * f + g + 1)
                dve.wait_ge(bank_free[g], f)
                if not isinstance(fu, int) or fu >= 2:
                    dve.wait_ge(f_lo, fu - 1)
                dve.tensor_tensor(h, banks[:, g, 0:G], Gt[:, b, g * G:(g + 1) * G], ALU.mult).then_inc(bank_free[g], 1)
                dve.wait_ge(f_hi, fu + 1)
                dve.tensor_tensor(acts[slot][:, b, 1, g * G:(g + 1) * G], h,
                                  acts[slot][:, b, 0, g * G:(g + 1) * G].bitcast(F32), ALU.subtract).then_inc(f_lo, 1)

            F0 = OUT_SLAB
            for g in range(NG):
                x = 2 * g + 1
                dve.wait_ge(gemm_ready, 3 * F0 + x + 1)
                dve.wait_ge(bank_free[(x - 1) % 3], F0 + (x - 1) // 3 + 1)
                if g == 2:
                    dve.wait_ge(f_lo, g - 1)
                dve.tensor_tensor(Ht[:, g % 2, :], banks[:, x % 3, 0:G], Gt[:, 0, g * G:(g + 1) * G], ALU.mult)\
                    .then_inc(bank_free[x % 3], 1)
                dve.wait_ge(f_hi, g + 1)
                dve.tensor_tensor(acts[0][:, 0, 1, g * G:(g + 1) * G], Ht[:, g % 2, :],
                                  acts[0][:, 0, 0, g * G:(g + 1) * G].bitcast(F32), ALU.subtract).then_inc(f_lo, 1)
                if g < 2:
                    norm_lo_part(1, 7 + g)
            for g in range(NG):
                up(F0 + 3, 0, 0, 0, 0, 1, g)
            with dve.Fori(0, (NCH - 1) // 2) as i:
                for odd in range(2):
                    for b in range(2):
                        for g in range(NG):
                            up(F0 + 4 + 4 * odd + 2 * b + 1, 8, i, 2 * i + 1 + odd, 1 - odd, b, g)
                    for hf in range(2):
                        add_rows(8 + 4 * i + 2 * odd + hf, hf)
            for hf in range(2):
                add_rows(8 + 2 * (NCH - 1) + hf, hf)

        @block.tensor
        def _(pe):
            def feature_unit(slot, free, g, hooks={}, bank=None):
                bank = g if bank is None else bank
                if free is not None:
                    pe.wait_ge(bank_free[bank], free)
                for kt in range(KT):
                    if kt in hooks:
                        hooks[kt]()
                    for n, (w, x) in enumerate(PASSES):
                        mm = pe.matmul(banks[:, bank, 0:G], ws[slot][w][:, kt * P:(kt + 1) * P],
                                       xs[x][:, kt, g * G:(g + 1) * G],
                                       start=(kt == 0 and n == 0), stop=(kt == KT - 1 and n == 2))
                mm.then_inc(gemm_ready, 1)

            def norm_transpose(ph, t):
                xn = (xn_p, xn_f)[ph]
                pe.wait_ge(xn_ready, NT * ph + t + 1)
                for h in range(2):
                    idx = 2 * t + h
                    if ph == 1 and t >= 7:
                        pe.wait_ge(d_free, 8 * NT)
                    elif idx >= 3:
                        pe.wait_ge(norm_lo, 2 * NT * ph + idx - 2)
                    for k in range(4):
                        kt = 4 * h + k
                        mm = pe.transpose(banks[:, norm_bank(ph, t, h), k * P:(k + 1) * P],
                                          xn[:, t % 2, kt * P:(kt + 1) * P], ident[:, :])
                    mm.then_inc(nT_done, 1)

            pe.wait_ge(consts_made, 10)

            def v_transpose(x):
                pe.wait_ge(bank_free[x % 3], x // 3 + 1)
                if x >= 2:
                    pe.wait_ge(v_done, x - 1)
                for t in range(3):
                    mm = pe.transpose(banks[:, 3 + x % 2, t * P:(t + 1) * P], S[:, x % 2, t * P:(t + 1) * P], ident[:, :])
                mm.then_inc(vt_ready, 1)

            def k_mean_square(w):
                pe.wait_ge(sq_done, NT + w + 1)
                if w < 2:
                    pe.wait_ge(v_done, 5 + w)
                else:
                    pe.wait_ge(k_sd, w - 1)
                pe.matmul(banks[:, 3 + w % 2, 0:G], blockones[:, :], S[:, w % 2, :], start=True, stop=True)\
                    .then_inc(k_ms, 1)

            for t in range(3):
                norm_transpose(0, t)
            for x in range(6):
                if x < 2:
                    pe.wait_ge(w_lo, x + 1)
                pe.wait_ge(norm_lo, 6 * (x // 2 + 1))
                feature_unit(x % 2, 1 if x >= 3 else None, x // 2, {4: lambda: v_transpose(x - 1)} if x else {}, x % 3)
                for t in {0: (3,), 1: (4, 5), 2: (6,), 3: (7, 8)}.get(x, ()):
                    norm_transpose(0, t)
            for a in range(2):
                pe.wait_ge(w_lo, 3 + a)
                for g in range(NG):
                    w = 3 * a + g
                    feature_unit(a, 2 + a, g, {3: (lambda: k_mean_square(w - 1)) if w else (lambda: v_transpose(5))})
            k_mean_square(5)

            with pe.Fori(0, 2) as i:
                for j in range(4):
                    n = Q_SLAB + 4 * i + j
                    pe.wait_ge(w_lo, n + 1)
                    for g in range(NG):
                        feature_unit(j % 2, n, g)

            pe.wait_ge(const_in, 16 * 15)
            pe.transpose(banks[:, 5, 0:P], rows_st, ident[:, :]).then_inc(smallT, 1)
            pe.transpose(banks[:, 5, P:P + 24], rows_cw, ident[0:24, 0:24]).then_inc(smallT, 1)
            for t in range(2):
                for a in range(2):
                    mm = pe.transpose(banks[:, 3, (2 * t + a) * P:(2 * t + a + 1) * P],
                                      kT[:, a, (NT - 1 + t) * P:(NT + t) * P], ident[:, :])
            mm.then_inc(kt_ready, 1)

            def s0(i, t):
                q, par = STEPS * i + t, t % 2
                pe.wait_ge(staged, q + 1)
                pe.wait_ge(cache_in[par], 32 * (4 * i + t // 2 + 1))
                if t:
                    pe.wait_ge(o_done, SLOTS * i + 3 * (t - 1) + 1)
                for h in range(4):
                    pe.matmul(banks[:, 7, 2 * h:2 * h + 2], sqst[:, h, :], ones2[:, :], start=True, stop=True)
                for s in range(2):
                    half = slice(HD * s, HD * (s + 1))
                    pe.matmul(banks[half, 7, 8:9], sqs[half, :, :].rearrange("p h c -> p (h c)"), ones2[half, s:s + 1],
                              start=True, stop=True)
                pe.transpose(banks[:, 7, P:2 * P], ck[:, par, :], ident[:, :]).then_inc(s0_done, 1)

            def s1(i, t, u):
                z, par = SLOTS * i + 3 * t + u, t % 2
                if 3 * t + u:
                    pe.wait_ge(exp_done, z)
                if u < 2:
                    half = slice(HD * u, HD * (u + 1))
                    for b in range(2):
                        if t:
                            edges = [a.rearrange("p h (c k) -> p h c k", k=HD)[:, :, 0:4:3, :]
                                     for a in (scores[:, 2 * b:2 * b + 2, :], mask[:, 1:3, :])]
                            pe.matmul(edges[0], halves[:, :], edges[1], start=True, stop=False, skip_group_check=True)
                        else:
                            for h in range(2):
                                pe.matmul(scores[:, 2 * b + h, :], halves[:, :], mask[:, 0, :], start=(h == 0),
                                          stop=False, skip_group_check=True)
                        for h in range(2):
                            mm = pe.matmul(scores[:, 2 * b + h, :], qst[half, par, 2 * b + h, :], kst[half, par, :],
                                           start=False, stop=(h == 1), skip_group_check=True)
                else:
                    pe.wait_ge(s0_used, STEPS * i + t + 1)
                    off = P - DEC_T - DEC_T * t
                    pe.matmul(scores[:, 0, P:2 * P], ones_row[:, :], window[:, off:off + P], start=True, stop=False,
                              skip_group_check=True)
                    for s in range(2):
                        half = slice(HD * s, HD * (s + 1))
                        for k, keys in enumerate((ks[half, par, :], ksmp[half, :])):
                            mm = pe.matmul(scores[half, 0, k * P:(k + 1) * P],
                                           qs[half, par, :, :].rearrange("p h c -> p (h c)"), keys,
                                           start=False, stop=(k == 1), skip_group_check=True)
                mm.then_inc(s1_done, 1)

            def s2(i, t, u):
                z = SLOTS * i + 3 * t + u
                pe.wait_ge(p_ready, z + 1)
                for k in range(2):
                    for h in range(4 if u < 2 else 1):
                        mm = pe.transpose(banks[:, 5 + k, h * P:(h + 1) * P], Pb[:, (3 * t + u) % 2, h, k * P:(k + 1) * P],
                                          ident[:, :])
                mm.then_inc(s2_done, 1)

            def s3(i, t, u, s0_before=None):
                z, par = SLOTS * i + 3 * t + u, t % 2
                pe.wait_ge(pt_ready, z + 1)
                if 3 * t + u:
                    pe.wait_ge(o_done, z)
                if s0_before is not None:
                    pe.wait_ge(s0_used, STEPS * i + s0_before + 1)
                for e in range(2):
                    half = slice(HD * e, HD * (e + 1))
                    if u < 2:
                        out = banks[half, 7, 0:2 * P]
                        for k in range(2):
                            mm = pe.matmul(out, vst[:, par, k, HD * u:HD * (u + 1)], PT[:, k, e:e + 3:2, :],
                                           start=(k == 0), stop=(k == 1))
                    else:
                        for s in range(2):
                            out = banks[half, 7, 2 * DEC_T * s:2 * DEC_T * (s + 1)]
                            for k, v in enumerate((cv[:, par, :], vsmp[:, :])):
                                rows = PT[:, k, 0, :].rearrange("p (s h c) -> p s h c", s=2, h=4)[:, s, e:e + 3:2, :]
                                mm = pe.matmul(out, v[:, HD * s:HD * (s + 1)], rows, start=(k == 0), stop=(k == 1))
                mm.then_inc(s3_done, 1)

            pe.wait_ge(masks_done, 13)
            pe.wait_ge(kout_done, 1)
            with pe.Fori(0, 2) as i:
                s0(i, 0)
                for t in range(STEPS):
                    f = PAIR_SLAB + 10 * i + t
                    for u in range(3):
                        before = None if 3 * t + u == 0 else ((t, u - 1) if u else (t - 1, 2))
                        s1(i, t, u)

                        def middle():
                            if before is not None:
                                s2(i, *before)
                            if u == 2 and t + 1 < STEPS:
                                s0(i, t + 1)

                        if u == 0:
                            pe.wait_ge(w_lo, f + 1)
                        feature_unit(t % 2, f, u, {4: middle})
                        if before is not None:
                            s0_before = t + 1 if u == 2 and t + 1 < STEPS else 0 if (t, u) == (0, 1) else None
                            s3(i, *before, s0_before)
                for jj in range(2):
                    f = PAIR_SLAB + 10 * i + 8 + jj
                    pe.wait_ge(w_lo, f + 1)
                    for g in range(NG):
                        last = {0: lambda: s2(i, STEPS - 1, 2), 4: lambda: s3(i, STEPS - 1, 2)}
                        feature_unit(jj, f, g, last if jj == 0 and g == 0 else {})
            with pe.Fori(2, 4) as i:
                for c in range(10):
                    f = PAIR_SLAB + 10 * i + c
                    pe.wait_ge(w_lo, f + 1)
                    for g in range(NG):
                        feature_unit(c % 2, f, g)

            pe.wait_ge(tail_step, 8)
            for h in range(2):
                pe.wait_ge(bank_free[h], OUT_SLAB)
                for k in range(4):
                    mm = pe.transpose(banks[0:2 + 2 * DEC_B, h, k * P:(k + 1) * P], tails[:, 4 * h + k, :], ident[:, :])
                mm.then_inc(tailsT, 1)

            def row_unit(bank, slot, act_slot, t):
                for k in range(2):
                    for n, (w, x) in enumerate(PASSES):
                        mm = pe.matmul(banks[:, bank, :], acts[act_slot][:, k, x, t * P:(t + 1) * P],
                                       ws[slot][w][:, k * 512:(k + 1) * 512],
                                       start=(k == 0 and n == 0), stop=(k == 1 and n == 2))
                mm.then_inc(d_ready, 1)

            def row_units(slot, s, act_slot):
                for t in range(NT):
                    if t >= DU:
                        pe.wait_ge(d_free, NT * s + t - DU + 1)
                    elif not isinstance(s, int) or s > 0:
                        pe.wait_ge(d_free, NT * (s - 1) + t + (DU if t + DU < NT else 0) + 1)
                    row_unit(3 + t % DU, slot, act_slot, t)

            for c in range(3):
                pe.wait_ge(m_lo, c + 1)
                for hf in range(2):
                    pe.wait_ge(w_lo, OUT_SLAB + 2 * c + hf + 1)
                    row_units(hf, 2 * c + hf, c % 2)
            pe.wait_ge(m_lo, 4)
            for n, (hf, t) in enumerate(LAST_ROWS):
                if n in (0, LEAD):
                    pe.wait_ge(w_lo, OUT_SLAB + 7 + (n > 0))
                pe.wait_ge(d_free, LAST_BASE + n - DU + 1 + (1 if n < DU - 1 else 0))
                row_unit(3 + n % DU, hf, 1, t)
                if hf == 1 and t >= 2:
                    norm_transpose(1, t - 2)

            F0 = OUT_SLAB
            for x in range(6):
                if x < 2:
                    pe.wait_ge(w_lo, FFN_SLAB + x + 1)
                pe.wait_ge(norm_lo, 2 * NT + (13 if x < 1 else 14 if x < 4 else 18))
                feature_unit(x % 2, F0 + x // 3, x // 2, {}, x % 3)
                if x in (1, 3):
                    norm_transpose(1, 7 + x // 2)
            for k in range(2, 4):
                pe.wait_ge(w_lo, FFN_SLAB + k + 1)
                for g in range(NG):
                    feature_unit(k % 2, F0 + k, g)
            with pe.Fori(0, (NCH - 1) // 2) as i:
                for odd in range(2):
                    n0 = FFN_SLAB + 4 + 6 * odd + 12 * i
                    f0 = F0 + 4 + 4 * odd + 8 * i
                    for k in range(4):
                        pe.wait_ge(w_lo, n0 + k + 1)
                        for g in range(NG):
                            feature_unit(k % 2, f0 + k, g)
                    pe.wait_ge(f_lo, 6 * (2 * i + odd + 1))
                    for hf in range(2):
                        pe.wait_ge(w_lo, n0 + 4 + hf + 1)
                        row_units(hf, 8 + 4 * i + 2 * odd + hf, odd)
            pe.wait_ge(f_lo, 6 * NCH)
            for hf in range(2):
                pe.wait_ge(w_lo, FFN_SLAB + 64 + hf + 1)
                row_units(hf, 8 + 2 * (NCH - 1) + hf, 0)


_INS = ["x_prompt", "x_sample", "state_conv", "cache_k", "cache_v", "norm_mix_w", "w_in", "conv_w", "q_norm_w",
        "k_norm_w", "sinks", "w_out", "norm_ffn_w", "w_gate", "w_up", "w_down"]
_OUTS = [("y_prompt", (1, SEQ, D)), ("y_sample", (DEC_B, DEC_T, D)), ("new_conv_prompt", (1, 1, 2, D)),
         ("new_k_prompt", (1, 1, P, NKV, HD)), ("new_v_prompt", (1, 1, P, NKV, HD)),
         ("new_conv_sample", (1, DEC_B, 2, D)), ("new_k_sample", (1, DEC_B, DEC_T, NKV, HD)),
         ("new_v_sample", (1, DEC_B, DEC_T, NKV, HD))]


def kernel(**inputs):
    from concourse import bacc
    from concourse.bass_utils import run_bass_kernel_spmd

    nc = bacc.Bacc("TRN2", target_bir_lowering=False, num_devices=1)
    arrays, io = {}, {}
    for name in _INS:
        a = np.ascontiguousarray(inputs[name])
        arrays[f"in_{name}"] = a
        io[name] = nc.dram_tensor(f"in_{name}", a.shape, mybir.dt.from_np(a.dtype), kind="ExternalInput").ap()
    for name, shape in _OUTS:
        io[name] = nc.dram_tensor(f"out_{name}", shape, F32, kind="ExternalOutput").ap()
    build(nc, io)
    r = run_bass_kernel_spmd(nc, [arrays], core_ids=[0])
    return tuple(r.results[0][f"out_{name}"] for name, _ in _OUTS)
```

```python
from contextlib import ExitStack

import numpy as np

import concourse.bass as bass
from concourse import mybir

F32, F32R, BF16 = mybir.dt.float32, mybir.dt.float32r, mybir.dt.bfloat16
ALU = mybir.AluOpType
ACT = mybir.ActivationFunctionType
AX_X = mybir.AxisListType.X

P = 128
D = 1024
SEQ = 1024
DEC_B, DEC_T = 8, 16
TOK = SEQ + DEC_B * DEC_T
NT = TOK // P
NG = 3
G = TOK // NG
KT = D // P
HD = 64
NH, NKV = D // HD, 4
NV = NKV * HD
D_FF = 2816
FC = 256
NCH = D_FF // FC
EPS = 1e-6
NEG = -1e30
H_OFF, B_OFF, C_OFF, Q_OFF = 0, D, 2 * D, 3 * D
K_OFF = 4 * D
V_OFF = K_OFF + NKV * HD
GC_OFF = V_OFF + NKV * HD
GA_OFF = GC_OFF + D
UP0 = 2 + SEQ
UW = UP0 + DEC_B * (2 + DEC_T)
SLAB = KT * P
V_LATE = 4
Q_SLAB = 4
PAIR_SLAB = 12
OUT_SLAB = 52
FEAT = 2
Q_FEAT, PAIR_FEAT, OUT_FEAT = Q_SLAB - FEAT, PAIR_SLAB - FEAT, OUT_SLAB - FEAT
FFN_SLAB = 60
STEPS = 8
SLOTS = 3 * STEPS
PASSES = ((0, 0), (0, 1), (1, 0))
DU = 5
XW_TILES = 6


LEAD = 3
LAST_ROWS = [(hf, t - LEAD * hf) for t in range(NT + LEAD) for hf in range(2) if 0 <= t - LEAD * hf < NT]
LAST_POS = {ht: n for n, ht in enumerate(LAST_ROWS)}
LAST_BASE = 6 * NT


def norm_bank(ph, t, h):
    if ph == 0:
        return 5 + (2 * t + h) % 3
    return (2 * t + h) % 3 if t < 7 else (5, 6, 7, 3)[2 * (t - 7) + h]


def turn_bank(x):
    return (x + 2) % NG


class Slab:

    def __init__(self, first, per=0, i=0):
        self.n = first + per * i
        self.slot = first % 2
        self.turn = first // 2 + (per // 2) * i


def build(nc, io):
    ctx = ExitStack()
    with ctx:
        def sb(name, shape, dt=F32):
            return ctx.enter_context(nc.sbuf_tensor(name, shape, dt))

        def sem(name):
            return ctx.enter_context(nc.semaphore(name))

        def overlay(name, nbytes, *groups):
            out = []
            for group in groups:
                with ExitStack() as inner:
                    out.append([inner.enter_context(nc.sbuf_tensor(n, s, d)) for n, s, d in group])
            ctx.enter_context(nc.sbuf_tensor(name, [P, nbytes // 4], F32))
            return out

        xs = [sb("x_hi", [P, KT, TOK], F32R), sb("x_lo", [P, KT, TOK], F32R)]
        ([O], [xn_f, scratch_f, wbc_f, Gt, Ht]) = overlay(
            "o_space", KT * TOK * 4,
            [("O", [P, KT, TOK], F32)],
            [("xn_f", [P, 2, D], F32), ("scratch_f", [P, D], F32), ("wbc_f", [P, D], F32),
             ("silu_gate", [P, 2, TOK], F32), ("ffn_h", [P, 2, G], F32)])
        ([X], [V, kT, q_hi, k_hi, vst, ck, cv, ks, ksmp, vsmp, qs, mask, window, halves, ones_row]) = overlay(
            "x_space", NT * D * 4,
            [("X", [P, NT, D], F32)],
            [("V", [P, NT + 1, NKV * HD], F32), ("kT", [P, 2, P + TOK], F32),
             ("q_hi", [P, 2, 4, P], F32R), ("k_hi", [P, 2, 2 * P], F32R), ("v_stage", [P, 2, 2, P], F32),
             ("cache_k_rows", [P, 2, P], F32), ("cache_v_rows", [P, 2, P], F32), ("cache_kT", [P, 2, P], F32),
             ("sample_kT", [P, P], F32), ("sample_v", [P, P], F32), ("q_sample", [P, 2, 2, 4, DEC_T], F32),
             ("mask", [2, 3, 2 * P], BF16), ("window", [1, 2 * P - DEC_T], BF16),
             ("halves", [2, P], BF16), ("ones_row", [1, P], BF16)])
        act_bytes = 2 * 2 * TOK * 4
        ([xn_p, scratch_p, wbc_p, blockones], [Pb, PT, sqst, sqs, q_lo, k_lo], [act0]) = overlay(
            "act0_space", act_bytes,
            [("xn_p", [P, 2, D], F32), ("scratch_p", [P, D], F32), ("wbc_p", [P, D], F32), ("blockones", [P, P], F32)],
            [("probs", [P, 2, 4, 2 * P], F32), ("probsT", [P, 2, 4, P], F32), ("q_sq", [P, 4, P], F32),
             ("q_sample_sq", [P, 2, 4, DEC_T], F32),
             ("q_lo", [P, 4, P], F32R), ("k_lo", [P, 2 * P], F32R)],
            [("act0", [P, 2, 2, TOK], F32R)])
        ([A, U, S, k_full], [act1]) = overlay(
            "act1_space", act_bytes,
            [("branch", [P, 2, TOK], F32), ("u", [P, UW], F32), ("gate", [P, 2, G], F32), ("k_full", [P, 2 * P], F32)],
            [("act1", [P, 2, 2, TOK], F32R)])
        acts = [act0, act1]
        raw = [sb(f"w_raw{i}", [P, SLAB]) for i in range(2)]
        ws = [[sb(f"w_hi{i}", [P, SLAB], F32R), sb(f"w_lo{i}", [P, SLAB], F32R)] for i in range(2)]
        ident = sb("ident", [P, P])
        ones2 = sb("ones2", [P, 2])
        ones1 = sb("ones1", [P, 1])
        tails = sb("tails", [P, KT, 2 + 2 * DEC_B])
        stT = sb("stT", [P, DEC_B, 2, KT])
        cwT = sb("cwT", [P, 3, KT])
        qnw = sb("qnw", [P, 1])
        knw = sb("knw", [P, 1])
        eps = sb("eps", [P, 1])
        sinkb = sb("sinkb", [P, NH])
        sinkS = sb("sinkS", [P, 2])
        neghalf = sb("neghalf", [P, 9])
        ss = sb("ss", [P, NT])
        sd = sb("sd", [P, NT])
        rms = sb("rms", [P, NT])
        ms = sb("ms", [P, 2, 9])
        rs = sb("rs", [P, 2, 9])
        soft = sb("soft", [P, 9, 4])
        kr = A[:, 0, :].rearrange("p (r g) -> p r g", r=NG)
        kout = A[:, 1, 0:4 * P].rearrange("p (t c) -> p t c", t=2)
        rows_st, rows_cw = A[:, 1, 4 * P:5 * P], A[0:24, 1, 5 * P:6 * P]
        tout = U[0:2 + 2 * DEC_B, 0:D]

        banks = ctx.enter_context(nc.psum_tensor("banks", [P, 8, 512], F32))
        scores = banks[:, 3:5, :].rearrange("p b (h k) -> p (b h) k", k=2 * P)

        const_in = sem("const_in")
        x_in = [sem(f"x_in{t}") for t in range(NT)]
        raw_in = [sem("raw_in0"), sem("raw_in1")]
        cache_in = [sem("cache_in0"), sem("cache_in1")]
        wbc_in = sem("wbc_in")
        consts_made = sem("consts_made")
        w_hi, w_lo = sem("w_hi_ready"), sem("w_lo_ready")
        sq_done, sd_done, rms_done, xn_ready = sem("sq_done"), sem("sd_done"), sem("rms_done"), sem("xn_ready")
        xw_ready = sem("xw_ready")
        nT_done, norm_hi, norm_lo = sem("nT_done"), sem("norm_hi"), sem("norm_lo")
        gemm_ready = sem("gemm_ready")
        bank_free = [sem(f"bank_free{g}") for g in range(NG)]
        smallT, small_done = sem("smallT"), sem("small_done")
        v_ready, v_half_used, v_done = sem("v_ready"), sem("v_half_used"), sem("v_done")
        k_ms, k_sd, k_rs = sem("k_ms"), sem("k_sd"), sem("k_rs")
        kt_ready, kout_done = sem("kt_ready"), sem("kout_done")
        pads_done, masks_done = sem("pads_done"), sem("masks_done")
        qs_staged, sq_staged, k_step = sem("qs_staged"), sem("sq_staged"), sem("k_step")
        qk_staged, v_staged = sem("qk_staged"), sem("v_staged")
        s0_done, s0_used, rs_ready = sem("s0_done"), sem("s0_used"), sem("rs_ready")
        s1_done, s2_done, s3_done = sem("scores_done"), sem("probsT_done"), sem("pv_done")
        soft_done, exp_done, p_ready = sem("soft_done"), sem("exp_done"), sem("p_ready")
        pt_ready, o_done = sem("pt_ready"), sem("o_done")
        conv_step, sg_used, merged = sem("conv_step"), sem("sg_used"), sem("merged")
        tail_step, tailsT, tout_done = sem("tail_step"), sem("tailsT"), sem("tout_done")
        m_hi, m_lo = sem("m_hi"), sem("m_lo")
        d_ready, d_free = sem("d_ready"), sem("d_free")
        f_hi, f_lo = sem("f_hi"), sem("f_lo")
        small_out, y_out = sem("small_out"), sem("y_out")
        kstore_out = sem("kstore_out")

        w_in = io["w_in"][0].rearrange("(k p) c -> p k c", p=P)
        w_q = io["w_in"][0][:, Q_OFF:Q_OFF + D].rearrange("(k p) (a s j d) -> p k a s j d", p=P, a=2, s=2, j=4)
        w_gate = io["w_gate"][0].rearrange("(k p) c -> p k c", p=P)
        w_up = io["w_up"][0].rearrange("(k p) c -> p k c", p=P)
        w_out = io["w_out"][0].rearrange("(k p) n -> p k n", p=P)
        w_down = io["w_down"][0].rearrange("(k p) n -> p k n", p=P)
        xp = io["x_prompt"][0].rearrange("(t p) d -> t p d", p=P)
        xsm = io["x_sample"].rearrange("b t d -> (b t) d")
        yp = io["y_prompt"][0].rearrange("(t p) d -> t p d", p=P)
        ysm = io["y_sample"].rearrange("b t d -> (b t) d")
        cache_k = io["cache_k"][0].rearrange("b n h d -> b n (h d)")
        cache_v = io["cache_v"][0].rearrange("b n h d -> b n (h d)")

        def slab_is_done(eng, kind, idx):
            if kind == "u":
                eng.wait_ge(gemm_ready, idx)
            elif kind == "du":
                eng.wait_ge(d_ready, idx)
            elif kind == "f":
                eng.wait_ge(gemm_ready, 3 * (idx + 1))
            else:
                eng.wait_ge(d_ready, NT * (idx + 1))

        block = ctx.enter_context(nc.Block())

        @block.sync
        def _(sp):
            def load(slab, halves_of):
                if not (isinstance(slab.n, int) and slab.n < 2):
                    sp.wait_ge(w_lo, slab.n - 1)
                for dst, src in halves_of:
                    sp.dma_start(dst, src).then_inc(raw_in[slab.slot], 16)

            def cols(slab, w, c0):
                dst = raw[slab.slot][:, :].rearrange("p (k c) -> p k c", k=KT)
                load(slab, [(dst[:, h:h + 4, :], w[:, h:h + 4, bass.ds(c0, P)]) for h in (0, 4)])

            def x_tile(t):
                sp.dma_start(X[:, t, :], xp[t] if t < NT - 1 else xsm).then_inc(x_in[t], 16)

            def v_half(slab):
                k0 = slab.n * KT // 2
                load(slab, [(raw[slab.slot][:, k * NV:(k + 2) * NV].rearrange("p (k c) -> p k c", k=2),
                             w_in[:, k0 + k:k0 + k + 2, V_OFF:V_OFF + NV]) for k in (0, 2)])

            x_tile(0)
            sp.dma_start(wbc_p[:, :], io["norm_mix_w"][0].partition_broadcast(P)).then_inc(wbc_in, 16)
            v_half(Slab(0))
            x_tile(1)
            v_half(Slab(1))
            for t in range(2, NT):
                x_tile(t)
            cols(Slab(2), w_in, K_OFF)
            cols(Slab(3), w_in, K_OFF + P)
            with sp.Fori(0, 2) as i:
                for j in range(4):
                    slab = Slab(Q_SLAB + j, 4, i)
                    dst = raw[slab.slot][:, :].rearrange("p (k s c) -> p k s c", k=KT, s=2)
                    load(slab, [(dst[:, :, h, :], w_q[:, :, bass.ds(i, 1), h, j, :].rearrange("p k a d -> p k (a d)"))
                                for h in range(2)])

            def pair_loads(i):
                for jj in range(2):
                    for c, off in enumerate((H_OFF, C_OFF, B_OFF, GC_OFF)):
                        cols(Slab(PAIR_SLAB + 4 * jj + c, 10, i), w_in, off + (2 * i + jj) * P)
                for jj in range(2):
                    cols(Slab(PAIR_SLAB + 8 + jj, 10, i), w_in, GA_OFF + (2 * i + jj) * P)

            with sp.Fori(0, 2) as i:
                pair_loads(i)
            with sp.Fori(2, 4) as i:
                pair_loads(i)

            def rows(slab, w, k0, hf):
                load(slab, [(raw[slab.slot][:, k * 512:(k + 1) * 512],
                             w[:, bass.ds(k0 + k, 1), hf * 512:(hf + 1) * 512].rearrange("p a c -> p (a c)"))
                            for k in range(2)])

            sp.wait_ge(o_done, 2 * SLOTS)
            sp.wait_ge(cache_in[0], 32 * (STEPS + 1))
            sp.wait_ge(small_out, 32)
            for t in range(NT):
                x_tile(t)
            for c in range(4):
                for hf in range(2):
                    rows(Slab(OUT_SLAB + 2 * c + hf), w_out, 2 * c, hf)
            sp.wait_ge(m_lo, 4)
            sp.dma_start(wbc_f[:, :], io["norm_ffn_w"][0].partition_broadcast(P)).then_inc(wbc_in, 16)

            def gate_up(first, per, i, c):
                for b in range(2):
                    cols(Slab(first + 2 * b, per, i), w_gate, c * FC + b * P)
                    cols(Slab(first + 2 * b + 1, per, i), w_up, c * FC + b * P)

            def down(first, per, i, c):
                for hf in range(2):
                    rows(Slab(first + hf, per, i), w_down, 2 * c, hf)

            gate_up(FFN_SLAB, 0, 0, 0)
            with sp.Fori(0, (NCH - 1) // 2) as i:
                gate_up(FFN_SLAB + 4, 12, i, 2 * i + 1)
                down(FFN_SLAB + 8, 12, i, 2 * i)
                gate_up(FFN_SLAB + 10, 12, i, 2 * i + 2)
                down(FFN_SLAB + 14, 12, i, 2 * i + 1)
            down(FFN_SLAB + 64, 0, 0, NCH - 1)
            for hf in range(2):
                for t in range(NT):
                    sp.wait_ge(d_free, NT * (8 + 2 * (NCH - 1) + hf) + t + 1)
                    dst = yp[t] if t < NT - 1 else ysm
                    sp.dma_start(dst[:, hf * 512:(hf + 1) * 512], X[:, t, hf * 512:(hf + 1) * 512]).then_inc(y_out, 16)
            sp.wait_ge(y_out, 16 * 2 * NT)

        @block.gpsimd
        def _(gp):
            gp.memset(ident[:, :], 0.0).then_inc(consts_made, 1)
            gp.wait_ge(consts_made, 1)
            gp.affine_select(out=ident[:, :], in_=ident[:, :], compare_op=ALU.not_equal, fill=1.0, base=0,
                             pattern=[[-1, P]], channel_multiplier=1).then_inc(consts_made, 1)
            gp.memset(eps[:, :], EPS).then_inc(consts_made, 1)
            gp.memset(blockones[:, :], 0.0).then_inc(consts_made, 1)
            gp.memset(ones2[:, :], 0.0).then_inc(consts_made, 1)
            gp.memset(neghalf[:, :], -0.5).then_inc(consts_made, 1)
            gp.memset(ones1[:, :], 1.0).then_inc(consts_made, 1)
            gp.wait_ge(consts_made, 7)
            for s in range(2):
                half = slice(HD * s, HD * (s + 1))
                gp.memset(blockones[half, half], 1.0).then_inc(consts_made, 1)
                gp.memset(ones2[half, s:s + 1], 1.0).then_inc(consts_made, 1)

            def split_lo(slab):
                gp.wait_ge(w_hi, slab.n + 1)
                gp.tensor_tensor(ws[slab.slot][1][:, :], raw[slab.slot][:, :], ws[slab.slot][0][:, :].bitcast(F32),
                                 ALU.subtract).then_inc(w_lo, 1)

            split_lo(Slab(0))
            split_lo(Slab(1))
            gp.dma_start(rows_st, io["state_conv"][0].rearrange("b r (j c) -> (b r j) c", c=P)).then_inc(const_in, 16)
            gp.dma_start(rows_cw, io["conv_w"][0].rearrange("w (j c) -> (w j) c", c=P)).then_inc(const_in, 16)
            for s in range(2):
                gp.dma_start(qnw[HD * s:HD * (s + 1), :], io["q_norm_w"].rearrange("a d -> d a")).then_inc(const_in, 16)
                gp.dma_start(knw[HD * s:HD * (s + 1), :], io["k_norm_w"].rearrange("a d -> d a")).then_inc(const_in, 16)
            gp.dma_start(sinkb[:, :], io["sinks"][0].partition_broadcast(P)).then_inc(const_in, 16)
            sink_rows = io["sinks"][0].rearrange("(a r) -> r a", a=2)
            for r in range(8):
                gp.dma_start(sinkS[DEC_T * r:DEC_T * (r + 1), :], sink_rows[r].partition_broadcast(DEC_T),
                             allow_slow_non_contiguous=True).then_inc(const_in, 16)
            split_lo(Slab(2))
            gp.wait_ge(norm_lo, 2 * NT)
            gp.memset(V[:, 0, :], 0.0).then_inc(pads_done, 1)
            for a in range(2):
                gp.memset(kT[:, a, 0:P], 0.0).then_inc(pads_done, 1)
            gp.memset(mask[:, :, :], 0.0).then_inc(masks_done, 1)
            gp.memset(halves[:, :], 1.0).then_inc(masks_done, 1)
            gp.memset(ones_row[:, :], 1.0).then_inc(masks_done, 1)
            gp.memset(window[:, :], NEG).then_inc(masks_done, 1)
            gp.wait_ge(masks_done, 4)
            for v in (1, 2):
                gp.affine_select(out=mask[:, v, :], in_=mask[:, v, :], compare_op=ALU.is_ge, fill=NEG, base=0,
                                 pattern=[[1, 2 * P]], channel_multiplier=-HD).then_inc(masks_done, 1)
            gp.affine_select(out=mask[:, 0, :], in_=mask[:, 0, :], compare_op=ALU.is_ge, fill=NEG, base=-P,
                             pattern=[[1, 2 * P]], channel_multiplier=0).then_inc(masks_done, 1)
            gp.affine_select(out=halves[:, :], in_=halves[:, :], compare_op=ALU.is_ge, fill=0.0, base=0,
                             pattern=[[1, P]], channel_multiplier=-HD).then_inc(masks_done, 1)
            gp.memset(window[:, P - DEC_T:P], 0.0).then_inc(masks_done, 1)
            gp.wait_ge(masks_done, 9)
            for v in range(3):
                gp.affine_select(out=mask[:, v, :], in_=mask[:, v, :], compare_op=ALU.is_ge, fill=NEG, base=3 * HD - 1,
                                 pattern=[[-1, 2 * P]], channel_multiplier=HD).then_inc(masks_done, 1)
            gp.affine_select(out=halves[:, :], in_=halves[:, :], compare_op=ALU.is_ge, fill=0.0, base=HD - 1,
                             pattern=[[-1, P]], channel_multiplier=HD).then_inc(masks_done, 1)
            split_lo(Slab(3))
            split_lo(Slab(4))
            gp.wait_ge(v_done, NT)
            gp.dma_start(io["new_v_prompt"][0, 0].rearrange("n h d -> n (h d)"), V[:, NT - 1, :]).then_inc(small_out, 16)
            gp.dma_start(io["new_v_sample"][0].rearrange("b n h d -> (b n) (h d)"), V[:, NT, :]).then_inc(small_out, 16)
            with gp.Fori(0, 2) as i:
                for j in range(4):
                    split_lo(Slab(Q_SLAB + j + 1, 4, i))

            def stage(i, t):
                par, q = t % 2, STEPS * i + t
                if t >= 1:
                    gp.wait_ge(qk_staged, q)
                    gp.wait_ge(s0_done, q)
                if t >= 2:
                    gp.wait_ge(s3_done, 3 * (q - 1))
                blocks = bass.ds(4 * i, 4)
                q_t = O[:, blocks, t * P:(t + 1) * P]
                gp.tensor_copy(q_hi[:, par, :, :], q_t)
                gp.tensor_tensor(sqst[:, :, :], q_t, q_t, ALU.mult)
                q_s = O[:, blocks, SEQ + t * DEC_T:SEQ + (t + 1) * DEC_T]
                for s in range(2):
                    own = ones2[:, s:s + 1].broadcast_to([P, 4 * DEC_T]).rearrange("p (h c) -> p h c", h=4)
                    gp.tensor_tensor(qs[:, par, s, :, :], q_s, own, ALU.mult).then_inc(qs_staged, 1)
                gp.wait_ge(qs_staged, 2 * q + 2)
                q_bd = qs[:, par, :, :, :].rearrange("p s h c -> p (s h c)")
                gp.tensor_tensor(sqs[:, :, :, :].rearrange("p s h c -> p (s h c)"), q_bd, q_bd, ALU.mult)\
                    .then_inc(sq_staged, 1)
                for dst in (k_hi[:, par, :], k_full[:, :]):
                    ins = gp.tensor_tensor(dst, kT[:, bass.ds(i, 1), t * P:(t + 2) * P].rearrange("p a k -> p (a k)"),
                                           qnw[:, :].broadcast_to([P, 2 * P]), ALU.mult)
                ins.then_inc(k_step, 1)
                if t >= 1:
                    gp.wait_ge(s1_done, 3 * (q - 1) + 2)
                gp.wait_ge(k_step, q + 1)
                gp.tensor_tensor(k_lo[:, :], k_full[:, :], k_hi[:, par, :].bitcast(F32), ALU.subtract)
                gp.tensor_tensor(q_lo[:, :, :], q_t, q_hi[:, par, :, :].bitcast(F32), ALU.subtract).then_inc(qk_staged, 1)
                gp.wait_ge(s0_used, q + 1)
                gp.tensor_tensor(rs[:, par, :], ms[:, par, :], neghalf[:, :], ALU.pow).then_inc(rs_ready, 1)
                if t == 0:
                    gp.tensor_tensor(ksmp[:, :], kT[:, bass.ds(i, 1), SEQ + P:SEQ + 2 * P].rearrange("p a k -> p (a k)"),
                                     qnw[:, :].broadcast_to([P, P]), ALU.mult)
                    gp.tensor_copy(vsmp[:, :], V[:, NT, bass.ds(i * P, P)])
                gp.tensor_copy(vst[:, par, :, :], V[:, t:t + 2, bass.ds(i * P, P)]).then_inc(v_staged, 1)

            for g in range(NG):
                gp.wait_ge(bank_free[g], Q_FEAT + 4)
            gp.wait_ge(pads_done, 3)
            gp.wait_ge(const_in, 16 * 15)
            gp.wait_ge(consts_made, 11)
            with gp.Fori(0, 2) as i:
                stage(i, 0)
                for t in range(STEPS):
                    split_lo(Slab(PAIR_SLAB + t + 1, 10, i))
                    if t + 1 < STEPS:
                        stage(i, t + 1)
                for jj in range(2):
                    split_lo(Slab(PAIR_SLAB + 9 + jj, 10, i))
            with gp.Fori(2, 4) as i:
                for c in range(10):
                    split_lo(Slab(PAIR_SLAB + c + 1, 10, i))
            gp.wait_ge(tout_done, 2)
            gp.dma_start(io["new_conv_prompt"][0, 0], tout[0:2, :]).then_inc(small_out, 16)
            gp.dma_start(io["new_conv_sample"][0].rearrange("b r c -> (b r) c"), tout[2:2 + 2 * DEC_B, :])\
                .then_inc(small_out, 16)
            for n in range(OUT_SLAB + 1, FFN_SLAB):
                split_lo(Slab(n))
            gp.wait_ge(wbc_in, 32)
            for t in range(XW_TILES):
                gp.wait_ge(d_free, LAST_BASE + LAST_POS[1, t] + 1)
                if t >= 2:
                    gp.wait_ge(nT_done, 2 * (NT + t - 1))
                gp.tensor_tensor(xn_f[:, t % 2, :], X[:, t, :], wbc_f[:, :], ALU.mult).then_inc(xw_ready, 1)
            for n in range(FFN_SLAB, FFN_SLAB + 4 + 1):
                split_lo(Slab(n))
            with gp.Fori(0, (NCH - 1) // 2) as i:
                for c in range(12):
                    split_lo(Slab(FFN_SLAB + 5 + c, 12, i))
            split_lo(Slab(FFN_SLAB + 65))
            gp.wait_ge(small_out, 64)

        @block.scalar
        def _(act):
            def split_hi(slab, *free):
                act.wait_ge(raw_in[slab.slot], 32 * (slab.turn + 1))
                if free:
                    slab_is_done(act, *free)
                act.activation(ws[slab.slot][0][:, :], raw[slab.slot][:, :], ACT.Copy).then_inc(w_hi, 1)

            def norm_stats(ph, t):
                if ph == 0:
                    act.wait_ge(x_in[t], 16)
                else:
                    act.wait_ge(d_free, LAST_BASE + LAST_POS[1, t] + 1)
                q = (NT + 6) * ph + t + 1
                act.wait_ge(sq_done, q)
                scratch = (scratch_p, scratch_f)[ph]
                act.activation(scratch[:, :], X[:, t, :], ACT.Square, accum_out=ss[:, t:t + 1]).then_inc(sq_done, 1)
                act.wait_ge(sq_done, q + 1)
                act.activation(sd[:, t:t + 1], ss[:, t:t + 1], ACT.Sqrt, bias=eps[:, :], scale=1.0 / D).then_inc(sd_done, 1)

            def norm_hi_part(ph, t):
                for h in range(2):
                    idx = 2 * (NT * ph + t) + h
                    act.wait_ge(nT_done, idx + 1)
                    src = banks[:, norm_bank(ph, t, h), :].rearrange("p (k c) -> p k c", k=4)
                    act.activation(xs[0][:, 4 * h:4 * h + 4, t * P:(t + 1) * P], src, ACT.Copy).then_inc(norm_hi, 1)

            act.wait_ge(consts_made, 11)
            act.activation(sd[:, 0:1], eps[:, :], ACT.Sqrt).then_inc(sq_done, 1)
            norm_stats(0, 0)
            split_hi(Slab(0))
            norm_stats(0, 1)

            def v_rows(t):
                act.wait_ge(v_ready, t + 1)
                act.activation(V[:, 1 + t, :], banks[:, t % DU, 0:NV], ACT.Copy).then_inc(v_done, 1)

            for t in range(NT):
                norm_hi_part(0, t)
                if t + 2 < NT:
                    norm_stats(0, t + 2)
                if t == 0:
                    split_hi(Slab(1))
                if 2 <= t < NT - V_LATE + 2:
                    v_rows(t - 2)
            act.wait_ge(v_half_used, 1)
            split_hi(Slab(2))
            for t in range(NT - V_LATE, NT):
                v_rows(t)
            split_hi(Slab(3))

            def k_root(w):
                act.wait_ge(k_ms, w + 1)
                if w >= 3:
                    act.wait_ge(bank_free[w % 3], 1)
                act.activation(kr[:, w % 3, :], banks[:, 3 + w % 2, 0:G], ACT.Sqrt, bias=eps[:, :],
                               scale=1.0 / HD).then_inc(k_sd, 1)

            for w in range(6):
                g = w % 3
                act.wait_ge(gemm_ready, w + 1)
                if w >= 2:
                    act.wait_ge(k_ms, w - 1)
                act.activation(S[:, w % 2, :], banks[:, g, 0:G], ACT.Square).then_inc(sq_done, 1)
                k_root(w)
                if w == 2:
                    split_hi(Slab(4), "f", 0)

            def cache_loads(i, t):
                for cache, dst in ((cache_k, ck), (cache_v, cv)):
                    act.dma_start(dst[:, t % 2, :], cache[t][:, bass.ds(i * P, P)]).then_inc(cache_in[t % 2], 16)

            act.wait_ge(norm_lo, 2 * NT)
            cache_loads(0, 0)
            with act.Fori(0, 2) as i:
                for j in range(4):
                    split_hi(Slab(Q_SLAB + j + 1, 4, i), "f", Q_FEAT + 4 * i + j - 1)
                    for g in range(NG):
                        act.wait_ge(gemm_ready, 3 * (Q_FEAT + 4 * i + j) + g + 1)
                        act.activation(O[:, bass.ds(4 * i + j, 1), g * G:(g + 1) * G].rearrange("p a c -> p (a c)"),
                                       banks[:, g, 0:G], ACT.Copy).then_inc(bank_free[g], 1)

            act.wait_ge(kout_done, 1)
            act.dma_start(io["new_k_prompt"][0, 0].rearrange("n h d -> n (h d)"), kout[:, 0, :]).then_inc(kstore_out, 16)
            act.dma_start(io["new_k_sample"][0].rearrange("b n h d -> (b n) (h d)"), kout[:, 1, :])\
                .then_inc(kstore_out, 16)

            def out_attention(i, t, u):
                z = SLOTS * i + 3 * t + u
                act.wait_ge(s3_done, z + 1)
                if u < 2:
                    dst = O[:, bass.ds(4 * i, 4), t * P:(t + 1) * P].rearrange("p (s b) q -> p s b q", s=2)[:, :, u, :]
                    src = banks[:, 7, 0:2 * P].rearrange("p (b q) -> p b q", b=2)
                else:
                    dst = O[:, bass.ds(4 * i, 4), SEQ + t * DEC_T:SEQ + (t + 1) * DEC_T]
                    src = banks[:, 7, 0:4 * DEC_T].rearrange("p (b q) -> p b q", b=4)
                act.activation(dst, src, ACT.Copy, scale=0.5).then_inc(o_done, 1)

            def exps(i, t, u):
                z, par = SLOTS * i + 3 * t + u, t % 2
                p = Pb[:, (3 * t + u) % 2]
                n = 4 if u < 2 else 1
                act.wait_ge(soft_done, 7 * z + 5)
                for h in range(n):
                    c = 4 * u + 2 * (h % 2) + h // 2 if u < 2 else 8
                    scale = rs[:, par, c:c + 1]
                    act.activation(p[:, h, :], scores[:, h, :], ACT.Exp, bias=soft[:, 3, h:h + 1], scale=scale,
                                   accum_out=soft[:, 5, h:h + 1])
                act.activation(soft[:, 6, 0:n], soft[:, 4, 0:n], ACT.Exp).then_inc(exp_done, 1)
                act.wait_ge(soft_done, 7 * z + 7)
                for h in range(n):
                    ins = act.activation(p[:, h, :], p[:, h, :], ACT.Copy, scale=soft[:, 8, h:h + 1])
                ins.then_inc(p_ready, 1)

            def unit(i, c, g):
                f = PAIR_FEAT + 10 * i + c
                bank = banks[:, g, 0:G]
                jj, kind = (c // 4, c % 4) if c < 8 else (c - 8, 4)
                if kind == 0:
                    act.wait_ge(gemm_ready, 3 * f + g + 1)
                    act.wait_ge(kstore_out, 32)
                    act.wait_ge(merged, 6 * i + 1)
                    act.activation(A[:, jj, g * G:(g + 1) * G], bank, ACT.Copy).then_inc(bank_free[g], 1)
                elif kind >= 3:
                    e = 12 * i + (3 * jj if kind == 3 else 6 + 3 * jj) + g
                    act.wait_ge(gemm_ready, 3 * f + g + 1)
                    slot = (3 * jj + g) % 2
                    if c > 3 or g > 1:
                        act.wait_ge(sg_used, e - 1)
                    act.activation(S[:, slot, :], bank, ACT.Tanh, scale=0.5).then_inc(bank_free[g], 1)

            with act.Fori(0, 2) as i:
                for t in range(STEPS):
                    split_hi(Slab(PAIR_SLAB + t + 1, 10, i), "f", PAIR_FEAT + 10 * i + t - 1)
                    for u in range(3):
                        exps(i, t, u)
                        unit(i, t, u)
                        if 3 * t + u:
                            out_attention(i, *((t, u - 1) if u else (t - 1, 2)))
                        if u == 0 and t + 1 < STEPS:
                            cache_loads(i, t + 1)
                split_hi(Slab(PAIR_SLAB + 9, 10, i), "f", PAIR_FEAT + 10 * i + 7)
                out_attention(i, STEPS - 1, 2)
                cache_loads(1, 0)
                for g in range(NG):
                    unit(i, 8, g)
                split_hi(Slab(PAIR_SLAB + 10, 10, i), "f", PAIR_FEAT + 10 * i + 8)
                for g in range(NG):
                    unit(i, 9, g)

            def merged_hi(c):
                act.wait_ge(merged, 1 + (6 * (c + 1) if c != 1 else 24))
                if c == 1:
                    act.wait_ge(small_out, 64)
                if c >= 2:
                    slab_is_done(act, "d", 2 * (c - 2) + 1)
                act.activation(acts[c % 2][:, :, 0, :], O[:, 2 * c:2 * c + 2, :], ACT.Copy).then_inc(m_hi, 1)

            merged_hi(0)
            with act.Fori(2, 4) as i:
                for c in range(10):
                    split_hi(Slab(PAIR_SLAB + c + 1, 10, i), "f", PAIR_FEAT + 10 * i + c - 1)
                    for g in range(NG):
                        unit(i, c, g)

            for c in range(4):
                for hf in range(2):
                    n = 2 * c + hf
                    if n < 7:
                        split_hi(Slab(OUT_SLAB + n + 1), *(("d", n - 1) if n else ("f", OUT_FEAT - 1)))
                    if hf == 0 and c < 3:
                        merged_hi(c + 1)

            def gate(first, per, i, b, g):
                f = first + per * i
                act.wait_ge(gemm_ready, 3 * f + g + 1)
                act.activation(Gt[:, b, g * G:(g + 1) * G], banks[:, g, 0:G], ACT.Silu).then_inc(bank_free[g], 1)

            def up(first, per, i, slot, b, g):
                f = first + per * i
                act.wait_ge(bank_free[g], f + 1)
                act.activation(acts[slot][:, b, 0, g * G:(g + 1) * G], Ht[:, (3 * b + g) % 2, :], ACT.Copy)\
                    .then_inc(f_hi, 1)

            F0 = OUT_FEAT
            act.wait_ge(m_lo, 4)
            for t in range(NT):
                if t == XW_TILES:
                    split_hi(Slab(FFN_SLAB), "du", LAST_BASE + LAST_POS[0, NT - 1] + 1)
                if t >= 2:
                    norm_hi_part(1, t - 2)
                norm_stats(1, t)
            split_hi(Slab(FFN_SLAB + 1), "d", 7)

            def gate_turn(g):
                x = 2 * g
                act.wait_ge(gemm_ready, 3 * F0 + x + 1)
                act.activation(Gt[:, 0, g * G:(g + 1) * G], banks[:, turn_bank(x), 0:G], ACT.Silu)\
                    .then_inc(bank_free[turn_bank(x)], 1)

            def up_turn(g):
                x = 2 * g
                act.wait_ge(bank_free[turn_bank(x + 1)], F0 + (x + 1) // 3 + 1)
                act.activation(acts[0][:, 0, 0, g * G:(g + 1) * G], Ht[:, g % 2, :], ACT.Copy).then_inc(f_hi, 1)

            gate_turn(0)
            norm_hi_part(1, 7)
            up_turn(0)
            norm_hi_part(1, 8)
            gate_turn(1)
            up_turn(1)
            gate_turn(2)
            split_hi(Slab(FFN_SLAB + 2), "u", 3 * F0 + 5)
            up_turn(2)
            split_hi(Slab(FFN_SLAB + 3), "f", F0 + 1)
            for g in range(NG):
                gate(F0 + 2, 0, 0, 1, g)
            split_hi(Slab(FFN_SLAB + 4), "f", F0 + 2)
            for g in range(NG):
                up(F0 + 3, 0, 0, 0, 1, g)

            with act.Fori(0, (NCH - 1) // 2) as i:
                for odd in range(2):
                    n0 = FFN_SLAB + 4 + 6 * odd
                    f0 = F0 + 4 + 4 * odd
                    s0 = 8 + 2 * odd
                    slot = 1 - odd
                    for b in range(2):
                        for k in range(2):
                            idx = 2 * b + k
                            if idx == 0:
                                if odd:
                                    free = ("d", s0 - 2 + 4 * i + 1)
                                else:
                                    free = None
                            else:
                                free = ("f", f0 + idx - 1 + 8 * i)
                            if free is None:
                                act.wait_ge(gemm_ready, 3 * (F0 + 4 + 8 * i))
                                act.wait_ge(d_ready, NT * (8 + 4 * i))
                                split_hi(Slab(n0 + 1, 12, i))
                            else:
                                split_hi(Slab(n0 + idx + 1, 12, i), *free)
                            for g in range(NG):
                                if k == 0:
                                    gate(f0 + idx, 8, i, b, g)
                                else:
                                    up(f0 + idx, 8, i, slot, b, g)
                    split_hi(Slab(n0 + 5, 12, i), "f", f0 + 3 + 8 * i)
                    split_hi(Slab(n0 + 6, 12, i), "d", s0 + 4 * i)
            split_hi(Slab(FFN_SLAB + 65), "d", 8 + 2 * (NCH - 1) - 1)

        @block.vector
        def _(dve):
            def norm_scale(ph, t):
                xn, wbc = ((xn_p, wbc_p), (xn_f, wbc_f))[ph]
                q = NT * ph + t
                dve.wait_ge(sd_done, q + 1)
                dve.reciprocal(rms[:, t:t + 1], sd[:, t:t + 1]).then_inc(rms_done, 1)
                if t >= 2:
                    dve.wait_ge(nT_done, 2 * (q - 1))
                dve.wait_ge(rms_done, q + 1)
                if ph == 1 and t < XW_TILES:
                    dve.wait_ge(xw_ready, t + 1)
                    dve.tensor_scalar(xn[:, t % 2, :], xn[:, t % 2, :], rms[:, t:t + 1], None, ALU.mult)\
                        .then_inc(xn_ready, 1)
                    return
                dve.scalar_tensor_tensor(out=xn[:, t % 2, :], in0=X[:, t, :], scalar=rms[:, t:t + 1], in1=wbc[:, :],
                                         op0=ALU.mult, op1=ALU.mult).then_inc(xn_ready, 1)

            def norm_lo_part(ph, t):
                for h in range(2):
                    idx = 2 * (NT * ph + t) + h
                    dve.wait_ge(norm_hi, idx + 1)
                    src = banks[:, norm_bank(ph, t, h), :].rearrange("p (k c) -> p k c", k=4)
                    where = (slice(None), slice(4 * h, 4 * h + 4), slice(t * P, (t + 1) * P))
                    dve.tensor_tensor(xs[1][where], src, xs[0][where].bitcast(F32), ALU.subtract).then_inc(norm_lo, 1)

            dve.wait_ge(wbc_in, 16)
            norm_scale(0, 0)
            norm_scale(0, 1)

            for t in range(NT):
                norm_lo_part(0, t)
                if t + 2 < NT:
                    norm_scale(0, t + 2)
            dve.wait_ge(const_in, 16 * 15)
            for w in range(6):
                a, g = divmod(w, 3)
                dve.wait_ge(k_sd, w + 1)
                dve.reciprocal(kr[:, w % 3, :], kr[:, w % 3, :]).then_inc(k_rs, 1)
                dve.wait_ge(k_rs, w + 1)
                dve.scalar_tensor_tensor(out=kT[:, a, P + g * G:P + (g + 1) * G], in0=banks[:, g, 0:G], scalar=knw[:, :],
                                         in1=kr[:, w % 3, :], op0=ALU.mult, op1=ALU.mult).then_inc(bank_free[g], 1)
            dve.wait_ge(smallT, 2)
            dve.tensor_copy(stT[:, :, :, :].rearrange("p b r j -> p (b r j)"), banks[:, 5, 0:P]).then_inc(small_done, 1)
            dve.tensor_scalar(cwT[:, :, :].rearrange("p w j -> p (w j)"), banks[:, 5, P:P + 24], 0.5, None, ALU.mult)\
                .then_inc(small_done, 1)
            dve.wait_ge(kt_ready, 1)
            dve.tensor_copy(kout[:, :, :].rearrange("p t c -> p (t c)"), banks[:, 6, :]).then_inc(kout_done, 1)

            def after_s0(i, t):
                q, par = STEPS * i + t, t % 2
                dve.wait_ge(s0_done, q + 1)
                dve.tensor_scalar(ms[:, par, :], banks[:, 7, 0:9], HD * EPS, None, ALU.add)
                dve.tensor_scalar(ks[:, par, :], banks[:, 7, P:2 * P], qnw[:, :], None, ALU.mult).then_inc(s0_used, 1)

            def out_transposed(i, t, u):
                z = SLOTS * i + 3 * t + u
                dve.wait_ge(s2_done, z + 1)
                n = 4 * P if u < 2 else P
                dst = PT[:, :, :, :].rearrange("p k h q -> p k (h q)")[:, :, 0:n]
                dve.tensor_copy(dst, banks[:, 5:7, 0:n]).then_inc(pt_ready, 1)

            def softmax_bias(i, t, u):
                z, par = SLOTS * i + 3 * t + u, t % 2
                n = 4 if u < 2 else 1
                if u < 2:
                    r = rs[:, par, 4 * u:4 * u + 4].rearrange("p (j s) -> p s j", s=2)
                    sink = sinkb[:, bass.ds(8 * i, 8)].rearrange("p (s j) -> p s j", s=2)[:, :, 2 * u:2 * u + 2]
                    st = [soft[:, k, 0:4].rearrange("p (s j) -> p s j", s=2) for k in range(9)]
                else:
                    r, sink = rs[:, par, 8:9], sinkS[:, bass.ds(i, 1)]
                    st = [soft[:, k, 0:1] for k in range(9)]
                dve.wait_ge(s1_done, z + 1)
                dve.tensor_reduce(soft[:, 0, 0:n], scores[:, 0:n, :], AX_X, ALU.max).then_inc(soft_done, 1)
                dve.wait_ge(rs_ready, STEPS * i + t + 1)
                dve.wait_ge(soft_done, 7 * z + 1)
                dve.tensor_tensor(st[1], st[0], r, ALU.mult).then_inc(soft_done, 1)
                dve.wait_ge(soft_done, 7 * z + 2)
                dve.tensor_tensor(st[2], st[1], sink, ALU.max).then_inc(soft_done, 1)
                dve.wait_ge(soft_done, 7 * z + 3)
                dve.tensor_scalar(soft[:, 3, 0:n], soft[:, 2, 0:n], -1.0, None, ALU.mult).then_inc(soft_done, 1)
                dve.wait_ge(soft_done, 7 * z + 4)
                dve.tensor_tensor(st[4], st[3], sink, ALU.add).then_inc(soft_done, 1)

            def denominator(i, t, u):
                z = SLOTS * i + 3 * t + u
                n = 4 if u < 2 else 1
                dve.wait_ge(exp_done, z + 1)
                dve.tensor_tensor(soft[:, 7, 0:n], soft[:, 5, 0:n], soft[:, 6, 0:n], ALU.add).then_inc(soft_done, 1)
                dve.wait_ge(soft_done, 7 * z + 6)
                dve.reciprocal(soft[:, 8, 0:n], soft[:, 7, 0:n]).then_inc(soft_done, 1)

            def u_parts(g):
                lo, hi = g * G, min((g + 1) * G, SEQ)
                return lo, hi

            def sample_view(buf, off):
                return buf[:, UP0:UW].rearrange("p (b c) -> p b c", b=DEC_B)[:, :, off:off + DEC_T]

            def sample_cols(a):
                return a[:, SEQ:TOK].rearrange("p (b c) -> p b c", b=DEC_B)

            def conv(i, jj, g):
                lo, hi = u_parts(g)
                base = 18 * i + 3 * (3 * jj + g)
                dve.wait_ge(bank_free[g], PAIR_FEAT + 10 * i + 4 * jj + 2)
                for k in range(3):
                    w = cwT[:, k, bass.ds(2 * i + jj, 1)]
                    if k:
                        dve.wait_ge(conv_step, base + k)
                    parts = [(A[:, jj, lo:hi], U[:, lo + k:hi + k])]
                    if g == 2:
                        parts.append((sample_cols(A[:, jj, :]), sample_view(U, k)))
                    for y, src in parts:
                        if k == 0:
                            ins = dve.tensor_scalar(y, src, w, None, ALU.mult)
                        else:
                            ins = dve.scalar_tensor_tensor(out=y, in0=src, scalar=w, in1=y, op0=ALU.mult, op1=ALU.add)
                    ins.then_inc(conv_step, 1)
                if g == 2:
                    j = bass.ds(2 * i + jj, 1)
                    dve.tensor_copy(tails[:, j, 0:2].rearrange("p a r -> p (a r)"), U[:, UP0 - 2:UP0])
                    dve.tensor_copy(tails[:, j, 2:].rearrange("p a (b r) -> p (a b) r", r=2),
                                    sample_view(U, 2)[:, :, DEC_T - 2:DEC_T]).then_inc(tail_step, 1)

            def unit(i, c, g):
                f = PAIR_FEAT + 10 * i + c
                bank = banks[:, g, 0:G]
                jj, kind = (c // 4, c % 4) if c < 8 else (c - 8, 4)
                a = A[:, jj, g * G:(g + 1) * G]
                if kind == 1:
                    lo, hi = u_parts(g)
                    if g == 0:
                        dve.tensor_copy(U[:, UP0:UW].rearrange("p (b c) -> p b c", b=DEC_B)[:, :, 0:2],
                                        stT[:, :, :, bass.ds(2 * i + jj, 1)].rearrange("p b r a -> p b (r a)"))
                    dve.wait_ge(gemm_ready, 3 * f + g + 1)
                    dve.wait_ge(bank_free[g], f)
                    ins = dve.tensor_tensor(U[:, 2 + lo:2 + hi], bank[:, 0:hi - lo], A[:, jj, lo:hi], ALU.mult)
                    if g == 2:
                        ins = dve.tensor_tensor(sample_view(U, 2),
                                                bank[:, hi - lo:G].rearrange("p (b c) -> p b c", b=DEC_B),
                                                sample_cols(A[:, jj, :]), ALU.mult)
                    ins.then_inc(bank_free[g], 1)
                elif kind == 2:
                    dve.wait_ge(gemm_ready, 3 * f + g + 1)
                    dve.wait_ge(conv_step, 18 * i + 9 * (jj + 1))
                    dve.tensor_tensor(a, bank, a, ALU.mult).then_inc(bank_free[g], 1)
                elif kind == 3:
                    dve.wait_ge(bank_free[g], f + 1)
                    dve.scalar_tensor_tensor(out=a, in0=S[:, (3 * jj + g) % 2, :], scalar=1.0, in1=a, op0=ALU.add,
                                             op1=ALU.mult).then_inc(sg_used, 1)
                elif kind == 4:
                    o = O[:, bass.ds(2 * i + jj, 1), g * G:(g + 1) * G].rearrange("p a c -> p (a c)")
                    e = 12 * i + 6 + 3 * jj + g
                    dve.wait_ge(bank_free[g], f + 1)
                    dve.wait_ge(o_done, SLOTS * min2(i))
                    dve.scalar_tensor_tensor(out=o, in0=S[:, (3 * jj + g) % 2, :], scalar=1.0, in1=o, op0=ALU.add,
                                             op1=ALU.mult).then_inc(sg_used, 1)
                    dve.wait_ge(sg_used, e + 1)
                    dve.tensor_tensor(o, o, a, ALU.add).then_inc(merged, 1)

            attention_on = [True]

            def min2(i):
                return i + 1 if attention_on[0] else 2

            dve.wait_ge(small_done, 2)
            dve.memset(U[:, 0:2], 0.0).then_inc(merged, 1)
            with dve.Fori(0, 2) as i:
                after_s0(i, 0)
                for t in range(STEPS):
                    for u in range(3):
                        softmax_bias(i, t, u)
                        if 3 * t + u:
                            bt, bu = (t, u - 1) if u else (t - 1, 2)
                            out_transposed(i, bt, bu)
                        if u == 2 and t + 1 < STEPS:
                            after_s0(i, t + 1)
                        denominator(i, t, u)
                        if 3 * t + u and bt % 4 == 1:
                            conv(i, bt // 4, bu)
                        unit(i, t, u)
                out_transposed(i, STEPS - 1, 2)
                for jj in range(2):
                    for g in range(NG):
                        unit(i, 8 + jj, g)
            attention_on[0] = False

            def merged_lo(c):
                dve.wait_ge(m_hi, c + 1)
                dve.tensor_tensor(acts[c % 2][:, :, 1, :], O[:, 2 * c:2 * c + 2, :],
                                  acts[c % 2][:, :, 0, :].bitcast(F32), ALU.subtract).then_inc(m_lo, 1)

            merged_lo(0)
            with dve.Fori(2, 4) as i:
                for c in range(10):
                    for g in range(NG):
                        unit(i, c, g)
                        if c % 4 == 1 and c < 8:
                            conv(i, c // 4, g)

            def add_rows(s, hf, x_turn=None):
                for t in range(NT):
                    x = X[:, t, hf * 512:(hf + 1) * 512]
                    dve.wait_ge(d_ready, NT * s + t + 1)
                    if x_turn is not None:
                        dve.wait_ge(x_in[t], x_turn)
                    else:
                        dve.wait_ge(d_free, NT * (s - 2) + t + 1)
                    dve.tensor_tensor(x, banks[:, 3 + t % DU, :], x, ALU.add).then_inc(d_free, 1)

            dve.wait_ge(tailsT, 2)
            for h in range(2):
                dve.tensor_copy(tout[:, h * 512:(h + 1) * 512], banks[0:2 + 2 * DEC_B, h, :]).then_inc(tout_done, 1)
            for c in range(3):
                add_rows(2 * c, 0, 32 if c == 0 else None)
                merged_lo(c + 1)
                add_rows(2 * c + 1, 1, 32 if c == 0 else None)

            dve.wait_ge(wbc_in, 32)
            for n, (hf, t) in enumerate(LAST_ROWS):
                x = X[:, t, hf * 512:(hf + 1) * 512]
                dve.wait_ge(d_ready, LAST_BASE + n + 1)
                dve.wait_ge(d_free, NT * (4 + hf) + t + 1)
                dve.tensor_tensor(x, banks[:, 3 + n % DU, :], x, ALU.add).then_inc(d_free, 1)
                if hf == 1 and t >= 1:
                    norm_scale(1, t - 1)
                if hf == 1 and t >= 2:
                    norm_lo_part(1, t - 2)
            norm_scale(1, NT - 1)

            def up(first, per, i, c, slot, b, g):
                f = first + per * i
                fu = 6 * c + 3 * b + g
                h = Ht[:, (3 * b + g) % 2, :]
                dve.wait_ge(gemm_ready, 3 * f + g + 1)
                dve.wait_ge(bank_free[g], f)
                if not isinstance(fu, int) or fu >= 2:
                    dve.wait_ge(f_lo, fu - 1)
                dve.tensor_tensor(h, banks[:, g, 0:G], Gt[:, b, g * G:(g + 1) * G], ALU.mult).then_inc(bank_free[g], 1)
                dve.wait_ge(f_hi, fu + 1)
                dve.tensor_tensor(acts[slot][:, b, 1, g * G:(g + 1) * G], h,
                                  acts[slot][:, b, 0, g * G:(g + 1) * G].bitcast(F32), ALU.subtract).then_inc(f_lo, 1)

            F0 = OUT_FEAT
            for g in range(NG):
                x = 2 * g + 1
                if g < 2:
                    norm_lo_part(1, 7 + g)
                dve.wait_ge(gemm_ready, 3 * F0 + x + 1)
                dve.wait_ge(bank_free[turn_bank(x - 1)], F0 + (x - 1) // 3 + 1)
                if g == 2:
                    dve.wait_ge(f_lo, g - 1)
                dve.tensor_tensor(Ht[:, g % 2, :], banks[:, turn_bank(x), 0:G], Gt[:, 0, g * G:(g + 1) * G], ALU.mult)\
                    .then_inc(bank_free[turn_bank(x)], 1)
                dve.wait_ge(f_hi, g + 1)
                dve.tensor_tensor(acts[0][:, 0, 1, g * G:(g + 1) * G], Ht[:, g % 2, :],
                                  acts[0][:, 0, 0, g * G:(g + 1) * G].bitcast(F32), ALU.subtract).then_inc(f_lo, 1)
            for g in range(NG):
                up(F0 + 3, 0, 0, 0, 0, 1, g)
            with dve.Fori(0, (NCH - 1) // 2) as i:
                for odd in range(2):
                    for b in range(2):
                        for g in range(NG):
                            up(F0 + 4 + 4 * odd + 2 * b + 1, 8, i, 2 * i + 1 + odd, 1 - odd, b, g)
                    for hf in range(2):
                        add_rows(8 + 4 * i + 2 * odd + hf, hf)
            for hf in range(2):
                add_rows(8 + 2 * (NCH - 1) + hf, hf)

        @block.tensor
        def _(pe):
            def feature_unit(slot, free, g, hooks={}, bank=None):
                bank = g if bank is None else bank
                if free is not None:
                    pe.wait_ge(bank_free[bank], free)
                for kt in range(KT):
                    if kt in hooks:
                        hooks[kt]()
                    for n, (w, x) in enumerate(PASSES):
                        mm = pe.matmul(banks[:, bank, 0:G], ws[slot][w][:, kt * P:(kt + 1) * P],
                                       xs[x][:, kt, g * G:(g + 1) * G],
                                       start=(kt == 0 and n == 0), stop=(kt == KT - 1 and n == 2))
                mm.then_inc(gemm_ready, 1)

            def norm_transpose(ph, t):
                xn = (xn_p, xn_f)[ph]
                pe.wait_ge(xn_ready, NT * ph + t + 1)
                for h in range(2):
                    idx = 2 * t + h
                    if ph == 1 and t >= 7:
                        pe.wait_ge(d_free, 8 * NT)
                    elif idx >= 3:
                        pe.wait_ge(norm_lo, 2 * NT * ph + idx - 2)
                    for k in range(4):
                        kt = 4 * h + k
                        mm = pe.transpose(banks[:, norm_bank(ph, t, h), k * P:(k + 1) * P],
                                          xn[:, t % 2, kt * P:(kt + 1) * P], ident[:, :])
                    mm.then_inc(nT_done, 1)

            pe.wait_ge(consts_made, 11)

            def v_unit(t, half):
                for k in range(KT // 2):
                    for n, (w, x) in enumerate(PASSES):
                        mm = pe.matmul(banks[:, t % DU, 0:NV], xs[x][:, 4 * half + k, t * P:(t + 1) * P],
                                       ws[half][w][:, k * NV:(k + 1) * NV],
                                       start=(half == 0 and k == 0 and n == 0), stop=(half == 1 and k == 3 and n == 2))
                return mm

            def k_mean_square(w):
                pe.wait_ge(sq_done, 1 + NT + w + 1)
                if w < 2:
                    pe.wait_ge(v_done, NT)
                else:
                    pe.wait_ge(k_sd, w - 1)
                pe.matmul(banks[:, 3 + w % 2, 0:G], blockones[:, :], S[:, w % 2, :], start=True, stop=True)\
                    .then_inc(k_ms, 1)

            norm_transpose(0, 0)
            norm_transpose(0, 1)
            for t in range(NT):
                pe.wait_ge(norm_lo, 2 * (t + 1))
                if t >= DU:
                    pe.wait_ge(v_done, t - DU + 1)
                if t < 2:
                    pe.wait_ge(w_lo, 1)
                mm = v_unit(t, 0)
                if t < NT - V_LATE:
                    if t == 0:
                        pe.wait_ge(w_lo, 2)
                    v_unit(t, 1).then_inc(v_ready, 1)
                elif t == NT - 1:
                    mm.then_inc(v_half_used, 1)
                if t + 2 < NT:
                    norm_transpose(0, t + 2)
            for t in range(NT - V_LATE, NT):
                v_unit(t, 1).then_inc(v_ready, 1)
            for a in range(2):
                pe.wait_ge(w_lo, 3 + a)
                for g in range(NG):
                    w = 3 * a + g
                    if a == 0:
                        pe.wait_ge(v_done, NT - 3 + g)
                    feature_unit(a, a or None, g, {3: lambda: k_mean_square(w - 1)} if w else {})
            k_mean_square(5)

            with pe.Fori(0, 2) as i:
                for j in range(4):
                    pe.wait_ge(w_lo, Q_SLAB + 4 * i + j + 1)
                    for g in range(NG):
                        feature_unit(j % 2, Q_FEAT + 4 * i + j, g)

            pe.wait_ge(const_in, 16 * 15)
            pe.transpose(banks[:, 5, 0:P], rows_st, ident[:, :]).then_inc(smallT, 1)
            pe.transpose(banks[:, 5, P:P + 24], rows_cw, ident[0:24, 0:24]).then_inc(smallT, 1)
            for t in range(2):
                for a in range(2):
                    mm = pe.transpose(banks[:, 6, (2 * t + a) * P:(2 * t + a + 1) * P],
                                      kT[:, a, (NT - 1 + t) * P:(NT + t) * P], ident[:, :])
            mm.then_inc(kt_ready, 1)

            def s0(i, t):
                q, par = STEPS * i + t, t % 2
                pe.wait_ge(sq_staged, q + 1)
                pe.wait_ge(cache_in[par], 32 * (4 * i + t // 2 + 1))
                if t:
                    pe.wait_ge(o_done, SLOTS * i + 3 * (t - 1) + 1)
                for h in range(4):
                    pe.matmul(banks[:, 7, 2 * h:2 * h + 2], sqst[:, h, :], ones2[:, :], start=True, stop=True)
                pe.matmul(banks[:, 7, 8:9], sqs[:, :, :, :].rearrange("p s h c -> p (s h c)"), ones1[:, :],
                          start=True, stop=True)
                pe.transpose(banks[:, 7, P:2 * P], ck[:, par, :], ident[:, :]).then_inc(s0_done, 1)

            def s1(i, t, u):
                z, par = SLOTS * i + 3 * t + u, t % 2
                if 3 * t + u:
                    pe.wait_ge(exp_done, z)
                if u < 2:
                    pe.wait_ge(qk_staged, STEPS * i + t + 1)
                    for s in range(2):
                        if t:
                            edges = [a.rearrange("p h (c k) -> p h c k", k=HD)[:, :, 0:4:3, :]
                                     for a in (scores[:, 2 * s:2 * s + 2, :], mask[:, 1:3, :])]
                            pe.matmul(edges[0], halves[:, :], edges[1], start=True, stop=False, skip_group_check=True)
                        else:
                            for jj in range(2):
                                pe.matmul(scores[:, 2 * s + jj, :], halves[:, :], mask[:, 0, :], start=(jj == 0),
                                          stop=False, skip_group_check=True)
                    for jj in range(2):
                        b = 2 * u + jj
                        for n, (q_part, k_part) in enumerate(((q_hi[:, par, b, :], k_hi[:, par, :]),
                                                              (q_hi[:, par, b, :], k_lo[:, :]),
                                                              (q_lo[:, b, :], k_hi[:, par, :]))):
                            for s in range(2):
                                half = slice(HD * s, HD * (s + 1))
                                mm = pe.matmul(scores[:, 2 * s + jj, :], q_part[half], k_part[half],
                                               start=False, stop=(jj == 1 and n == 2), skip_group_check=True)
                else:
                    pe.wait_ge(s0_used, STEPS * i + t + 1)
                    pe.wait_ge(v_staged, STEPS * i + t + 1)
                    off = P - DEC_T - DEC_T * t
                    pe.matmul(scores[:, 0, P:2 * P], ones_row[:, :], window[:, off:off + P], start=True, stop=False,
                              skip_group_check=True)
                    for k, keys in enumerate((ks[:, par, :], ksmp[:, :])):
                        mm = pe.matmul(scores[:, 0, k * P:(k + 1) * P],
                                       qs[:, par, :, :, :].rearrange("p s h c -> p (s h c)"), keys,
                                       start=False, stop=(k == 1), skip_group_check=True)
                mm.then_inc(s1_done, 1)

            def s2(i, t, u):
                z = SLOTS * i + 3 * t + u
                pe.wait_ge(p_ready, z + 1)
                for k in range(2):
                    for h in range(4 if u < 2 else 1):
                        mm = pe.transpose(banks[:, 5 + k, h * P:(h + 1) * P], Pb[:, (3 * t + u) % 2, h, k * P:(k + 1) * P],
                                          ident[:, :])
                mm.then_inc(s2_done, 1)

            def s3(i, t, u, s0_before=None):
                z, par = SLOTS * i + 3 * t + u, t % 2
                pe.wait_ge(v_staged, STEPS * i + t + 1)
                pe.wait_ge(pt_ready, z + 1)
                if 3 * t + u:
                    pe.wait_ge(o_done, z)
                if s0_before is not None:
                    pe.wait_ge(s0_used, STEPS * i + s0_before + 1)
                if u < 2:
                    for s in range(2):
                        for k in range(2):
                            for e in range(2):
                                mm = pe.matmul(banks[HD * e:HD * (e + 1), 7, s * P:(s + 1) * P],
                                               vst[:, par, k, HD * s:HD * (s + 1)], PT[:, k, 2 * s + e, :],
                                               start=(k == 0), stop=(k == 1))
                else:
                    for e in range(2):
                        half = slice(HD * e, HD * (e + 1))
                        for s in range(2):
                            out = banks[half, 7, 2 * DEC_T * s:2 * DEC_T * (s + 1)]
                            for k, v in enumerate((cv[:, par, :], vsmp[:, :])):
                                rows = PT[:, k, 0, :].rearrange("p (s h c) -> p s h c", s=2, h=4)[:, s, e:e + 3:2, :]
                                mm = pe.matmul(out, v[:, HD * s:HD * (s + 1)], rows, start=(k == 0), stop=(k == 1))
                mm.then_inc(s3_done, 1)

            pe.wait_ge(masks_done, 13)
            with pe.Fori(0, 2) as i:
                s0(i, 0)
                for t in range(STEPS):
                    f = PAIR_FEAT + 10 * i + t
                    for u in range(3):
                        before = None if 3 * t + u == 0 else ((t, u - 1) if u else (t - 1, 2))
                        s1(i, t, u)

                        def middle():
                            if before is not None:
                                s2(i, *before)
                            if u == 2 and t + 1 < STEPS:
                                s0(i, t + 1)

                        if u == 0:
                            pe.wait_ge(w_lo, FEAT + f + 1)
                        feature_unit(t % 2, f, u, {4: middle})
                        if before is not None:
                            s0_before = t + 1 if u == 2 and t + 1 < STEPS else 0 if (t, u) == (0, 1) else None
                            s3(i, *before, s0_before)
                for jj in range(2):
                    f = PAIR_FEAT + 10 * i + 8 + jj
                    pe.wait_ge(w_lo, FEAT + f + 1)
                    for g in range(NG):
                        last = {0: lambda: s2(i, STEPS - 1, 2), 4: lambda: s3(i, STEPS - 1, 2)}
                        feature_unit(jj, f, g, last if jj == 0 and g == 0 else {})
            with pe.Fori(2, 4) as i:
                for c in range(10):
                    f = PAIR_FEAT + 10 * i + c
                    pe.wait_ge(w_lo, FEAT + f + 1)
                    for g in range(NG):
                        feature_unit(c % 2, f, g)

            pe.wait_ge(tail_step, 8)
            for h in range(2):
                pe.wait_ge(bank_free[h], OUT_FEAT)
                for k in range(4):
                    mm = pe.transpose(banks[0:2 + 2 * DEC_B, h, k * P:(k + 1) * P], tails[:, 4 * h + k, :], ident[:, :])
                mm.then_inc(tailsT, 1)

            def row_unit(bank, slot, act_slot, t):
                for k in range(2):
                    for n, (w, x) in enumerate(PASSES):
                        mm = pe.matmul(banks[:, bank, :], acts[act_slot][:, k, x, t * P:(t + 1) * P],
                                       ws[slot][w][:, k * 512:(k + 1) * 512],
                                       start=(k == 0 and n == 0), stop=(k == 1 and n == 2))
                mm.then_inc(d_ready, 1)

            def row_units(slot, s, act_slot):
                for t in range(NT):
                    if t >= DU:
                        pe.wait_ge(d_free, NT * s + t - DU + 1)
                    elif not isinstance(s, int) or s > 0:
                        pe.wait_ge(d_free, NT * (s - 1) + t + (DU if t + DU < NT else 0) + 1)
                    row_unit(3 + t % DU, slot, act_slot, t)

            for c in range(3):
                pe.wait_ge(m_lo, c + 1)
                for hf in range(2):
                    pe.wait_ge(w_lo, OUT_SLAB + 2 * c + hf + 1)
                    row_units(hf, 2 * c + hf, c % 2)
            pe.wait_ge(m_lo, 4)
            for n, (hf, t) in enumerate(LAST_ROWS):
                if n in (0, LEAD):
                    pe.wait_ge(w_lo, OUT_SLAB + 7 + (n > 0))
                pe.wait_ge(d_free, LAST_BASE + n - DU + 1 + (1 if n < DU - 1 else 0))
                row_unit(3 + n % DU, hf, 1, t)
                if hf == 1 and t >= 2:
                    norm_transpose(1, t - 2)

            F0 = OUT_FEAT
            for x in range(6):
                if x < 2:
                    pe.wait_ge(w_lo, FFN_SLAB + x + 1)
                pe.wait_ge(norm_lo, 2 * NT + (12 + min(x, 2) if x < 4 else 18))
                feature_unit(x % 2, F0 + x // 3, x // 2, {}, turn_bank(x))
                if x < 2:
                    norm_transpose(1, 7 + x)
            for k in range(2, 4):
                pe.wait_ge(w_lo, FFN_SLAB + k + 1)
                for g in range(NG):
                    feature_unit(k % 2, F0 + k, g)
            with pe.Fori(0, (NCH - 1) // 2) as i:
                for odd in range(2):
                    n0 = FFN_SLAB + 4 + 6 * odd + 12 * i
                    f0 = F0 + 4 + 4 * odd + 8 * i
                    for k in range(4):
                        pe.wait_ge(w_lo, n0 + k + 1)
                        for g in range(NG):
                            feature_unit(k % 2, f0 + k, g)
                    pe.wait_ge(f_lo, 6 * (2 * i + odd + 1))
                    for hf in range(2):
                        pe.wait_ge(w_lo, n0 + 4 + hf + 1)
                        row_units(hf, 8 + 4 * i + 2 * odd + hf, odd)
            pe.wait_ge(f_lo, 6 * NCH)
            for hf in range(2):
                pe.wait_ge(w_lo, FFN_SLAB + 64 + hf + 1)
                row_units(hf, 8 + 2 * (NCH - 1) + hf, 0)


_INS = ["x_prompt", "x_sample", "state_conv", "cache_k", "cache_v", "norm_mix_w", "w_in", "conv_w", "q_norm_w",
        "k_norm_w", "sinks", "w_out", "norm_ffn_w", "w_gate", "w_up", "w_down"]
_OUTS = [("y_prompt", (1, SEQ, D)), ("y_sample", (DEC_B, DEC_T, D)), ("new_conv_prompt", (1, 1, 2, D)),
         ("new_k_prompt", (1, 1, P, NKV, HD)), ("new_v_prompt", (1, 1, P, NKV, HD)),
         ("new_conv_sample", (1, DEC_B, 2, D)), ("new_k_sample", (1, DEC_B, DEC_T, NKV, HD)),
         ("new_v_sample", (1, DEC_B, DEC_T, NKV, HD))]


def kernel(**inputs):
    from concourse import bacc
    from concourse.bass_utils import run_bass_kernel_spmd

    nc = bacc.Bacc("TRN2", target_bir_lowering=False, num_devices=1)
    arrays, io = {}, {}
    for name in _INS:
        a = np.ascontiguousarray(inputs[name])
        arrays[f"in_{name}"] = a
        io[name] = nc.dram_tensor(f"in_{name}", a.shape, mybir.dt.from_np(a.dtype), kind="ExternalInput").ap()
    for name, shape in _OUTS:
        io[name] = nc.dram_tensor(f"out_{name}", shape, F32, kind="ExternalOutput").ap()
    build(nc, io)
    r = run_bass_kernel_spmd(nc, [arrays], core_ids=[0])
    return tuple(r.results[0][f"out_{name}"] for name, _ in _OUTS)
```
